# Optimizing a Trainium2 kernel written in Bass

```python
import math
import jax, jax.numpy as jnp
from jax import lax
import numpy as np

D_MODEL = 1024
BATCH = 1
SEQ = 512
DEPTH = 2
DEC_BATCH = 1
DEC_SEQ = 32
PAST_LEN = 128

CHUNK = 64
Q_BLOCK = 128
CONV_W = 512
CONV_K = 3
POOL_W = 512
POOL_GROUPS = 4
POOL_GC = POOL_W // POOL_GROUPS
POOL_WINDOWS = (2, 4, 8, 16)
POOL_HIST = 15
POOL_OUT = D_MODEL // POOL_GROUPS
HEADS_C = 4
HEAD_DIM_C = 64
ATT_W = HEADS_C * 2 * HEAD_DIM_C
N_BRANCH = 3
IN_COLS = 3 * CONV_W + POOL_W + 3 * ATT_W + N_BRANCH * D_MODEL
ROPE_THETA = 10000.0
D_FF = 2816
N_EXPERTS = 8
TOP_K = 2
D_FF_EXPERT = 1408
N_DENSE = (DEPTH + 1) // 2
N_MOE = DEPTH // 2
EPS = 1e-6
SUBLN_EPS = 1e-5

kernel_name = 'hybrid_streaming_encoder_step'

def rmsnorm(x, g, eps=EPS):
    xf = x.astype(jnp.float32)
    y = xf * lax.rsqrt(jnp.mean(xf * xf, axis=-1, keepdims=True) + eps)
    return (y * g.astype(jnp.float32)).astype(x.dtype)

def rope(x, pos):
    half = HEAD_DIM_C // 2
    inv_freq = ROPE_THETA ** (-jnp.arange(half, dtype=jnp.float32) / half)
    ang = pos.astype(jnp.float32)[:, None] * inv_freq[None, :]
    cos = jnp.cos(ang)[None, :, None, None, :]
    sin = jnp.sin(ang)[None, :, None, None, :]
    xf = x.astype(jnp.float32)
    x1, x2 = xf[..., :half], xf[..., half:]
    return jnp.concatenate([x1 * cos - x2 * sin, x2 * cos + x1 * sin], axis=-1).astype(x.dtype)

def causal_conv(ext, w, T):
    y = ext[:, 0:T] * w[0]
    for j in range(1, CONV_K):
        y = y + ext[:, j:j + T] * w[j]
    return y

def multiscale_pool(u_ext, pos):
    T = pos.shape[0]
    uf = u_ext.astype(jnp.float32)
    cs = jnp.cumsum(uf, axis=1)
    cs = jnp.concatenate([jnp.zeros_like(cs[:, :1]), cs], axis=1)
    cur = uf[:, POOL_HIST:]
    outs = []
    for gi, win in enumerate(POOL_WINDOWS):
        lo, hi = gi * POOL_GC, (gi + 1) * POOL_GC
        s = cs[:, POOL_HIST + 1:POOL_HIST + 1 + T, lo:hi] - cs[:, POOL_HIST + 1 - win:POOL_HIST + 1 - win + T, lo:hi]
        cnt = jnp.minimum(pos + 1, win).astype(jnp.float32)[None, :, None]
        outs.append(s / cnt - cur[..., lo:hi])
    return jnp.concatenate(outs, axis=-1).astype(u_ext.dtype)

def diff_attn_block(q, k, v, q_chunk, k_chunk, lam):
    scale = HEAD_DIM_C ** -0.5
    s = jnp.einsum('bqhcd,bkhcd->bhcqk', q.astype(jnp.float32), k.astype(jnp.float32)) * scale
    visible = k_chunk[None, :] <= q_chunk[:, None]
    s = jnp.where(visible, s, -jnp.inf)
    p = jax.nn.softmax(s, axis=-1)
    a = p[:, :, 0] - lam * p[:, :, 1]
    return jnp.einsum('bhqk,bkhe->bqhe', a, v.astype(jnp.float32))

def token_mixer(x, pos, conv_prev, pool_prev, k_past, v_past, layer,
                norm_g, w_in, conv_w, w_a, w_pool, pool_scale,
                lq1, lk1, lq2, lk2, subln_g, w_c, w_o):
    B, T, _ = x.shape
    h = rmsnorm(x, norm_g)
    z = jnp.einsum('btd,de->bte', h, w_in)
    cuts = [int(c) for c in np.cumsum([CONV_W, CONV_W, CONV_W, POOL_W, ATT_W, ATT_W, ATT_W])]
    xa, ba, ca, u, q, k, v, g = jnp.split(z, cuts, axis=-1)
    cin = ca * xa
    cext = jnp.concatenate([conv_prev.astype(cin.dtype), cin], axis=1)
    y_a = jnp.einsum('btc,cd->btd', ba * causal_conv(cext, conv_w, T), w_a)
    new_conv = cext[:, -(CONV_K - 1):]
    uext = jnp.concatenate([pool_prev.astype(u.dtype), u], axis=1)
    pooled = multiscale_pool(uext, pos).reshape(B, T, POOL_GROUPS, POOL_GC)
    y_b = jnp.einsum('btgc,gce->btge', pooled, w_pool).reshape(B, T, D_MODEL) * pool_scale
    new_pool = uext[:, -POOL_HIST:]
    q = rope(q.reshape(B, T, HEADS_C, 2, HEAD_DIM_C), pos)
    k = rope(k.reshape(B, T, HEADS_C, 2, HEAD_DIM_C), pos)
    v = v.reshape(B, T, HEADS_C, 2 * HEAD_DIM_C)
    k_new = k.reshape(B, T, HEADS_C, 2 * HEAD_DIM_C)
    q_chunk = pos // CHUNK
    lam_init = 0.8 - 0.6 * math.exp(-0.3 * layer)
    lam = (jnp.exp(jnp.sum(lq1.astype(jnp.float32) * lk1.astype(jnp.float32)))
           - jnp.exp(jnp.sum(lq2.astype(jnp.float32) * lk2.astype(jnp.float32))) + lam_init)
    if k_past is None:
        nb = T // Q_BLOCK
        qb = jnp.moveaxis(q.reshape(B, nb, Q_BLOCK, HEADS_C, 2, HEAD_DIM_C), 1, 0)
        cb = q_chunk.reshape(nb, Q_BLOCK)
        o = lax.map(lambda qc: diff_attn_block(qc[0], k, v, qc[1], q_chunk, lam), (qb, cb))
        o = jnp.moveaxis(o, 0, 1).reshape(B, T, HEADS_C, 2 * HEAD_DIM_C)
    else:
        P = k_past.shape[1]
        keys = jnp.concatenate([k_past.astype(k.dtype).reshape(B, P, HEADS_C, 2, HEAD_DIM_C), k], axis=1)
        vals = jnp.concatenate([v_past.astype(v.dtype), v], axis=1)
        k_chunk = jnp.concatenate([jnp.arange(P) // CHUNK, q_chunk])
        o = diff_attn_block(q, keys, vals, q_chunk, k_chunk, lam)
    o = rmsnorm(o, subln_g, SUBLN_EPS) * (1.0 - lam_init)
    y_c = jnp.einsum('bte,ed->btd', o.reshape(B, T, ATT_W).astype(x.dtype), w_c)
    gates = jax.nn.sigmoid(g.astype(jnp.float32)).astype(x.dtype).reshape(B, T, N_BRANCH, D_MODEL)
    merged = gates[:, :, 0] * y_a + gates[:, :, 1] * y_b + gates[:, :, 2] * y_c
    out = x + jnp.einsum('btd,de->bte', merged, w_o)
    return out, new_conv, new_pool, k_new, v

def swiglu(h, wg, wu, wd):
    a = jax.nn.silu(jnp.einsum('btd,df->btf', h, wg)) * jnp.einsum('btd,df->btf', h, wu)
    return jnp.einsum('btf,fd->btd', a, wd)

def moe_swiglu(h, w_r, b_r, wg, wu, wd):
    logits = jnp.einsum('btd,de->bte', h.astype(jnp.float32), w_r.astype(jnp.float32)) + b_r.astype(jnp.float32)
    top_val, top_idx = lax.top_k(logits, TOP_K)
    top_w = jax.nn.softmax(top_val, axis=-1)
    y = jnp.zeros_like(h)
    for e in range(N_EXPERTS):
        w_e = jnp.sum(jnp.where(top_idx == e, top_w, 0.0), axis=-1, keepdims=True).astype(h.dtype)
        y = y + w_e * swiglu(h, wg[e], wu[e], wd[e])
    return y

def channel_mixer(x, layer, norm_g, w_gate_d, w_up_d, w_down_d,
                  w_router, b_router, w_gate_e, w_up_e, w_down_e):
    h = rmsnorm(x, norm_g)
    if layer % 2 == 0:
        d = layer // 2
        return x + swiglu(h, w_gate_d[d], w_up_d[d], w_down_d[d])
    m = layer // 2
    return x + moe_swiglu(h, w_router[m], b_router[m], w_gate_e[m], w_up_e[m], w_down_e[m])

def setup_inputs(seed: int = 0) -> dict:
    key = jax.random.key(seed)
    ks = jax.random.split(key, 32)

    def nrm(k, shape, scale):
        return jax.random.normal(k, shape, jnp.float32) * scale

    return {
        'x_prompt': nrm(ks[0], (BATCH, SEQ, D_MODEL), 1.0),
        'x_sample': nrm(ks[1], (DEC_BATCH, DEC_SEQ, D_MODEL), 1.0),
        'cache_k': nrm(ks[2], (DEPTH, DEC_BATCH, PAST_LEN, HEADS_C, 2 * HEAD_DIM_C), 1.0),
        'cache_v': nrm(ks[3], (DEPTH, DEC_BATCH, PAST_LEN, HEADS_C, 2 * HEAD_DIM_C), 1.0),
        'state_conv': nrm(ks[4], (DEPTH, DEC_BATCH, CONV_K - 1, CONV_W), 1.0),
        'state_pool': nrm(ks[5], (DEPTH, DEC_BATCH, POOL_HIST, POOL_W), 1.0),
        'norm_mix': 1.0 + nrm(ks[6], (DEPTH, D_MODEL), 0.05),
        'w_in': nrm(ks[7], (DEPTH, D_MODEL, IN_COLS), D_MODEL ** -0.5),
        'conv_w': nrm(ks[8], (DEPTH, CONV_K, CONV_W), CONV_K ** -0.5),
        'w_conv_out': nrm(ks[9], (DEPTH, CONV_W, D_MODEL), CONV_W ** -0.5),
        'w_pool': nrm(ks[10], (DEPTH, POOL_GROUPS, POOL_GC, POOL_OUT), POOL_GC ** -0.5),
        'pool_scale': 1.0 + nrm(ks[11], (DEPTH, D_MODEL), 0.05),
        'lambda_q1': nrm(ks[12], (DEPTH, HEAD_DIM_C), 0.1),
        'lambda_k1': nrm(ks[13], (DEPTH, HEAD_DIM_C), 0.1),
        'lambda_q2': nrm(ks[14], (DEPTH, HEAD_DIM_C), 0.1),
        'lambda_k2': nrm(ks[15], (DEPTH, HEAD_DIM_C), 0.1),
        'subln_g': 1.0 + nrm(ks[16], (DEPTH, 2 * HEAD_DIM_C), 0.05),
        'w_attn_out': nrm(ks[17], (DEPTH, ATT_W, D_MODEL), ATT_W ** -0.5),
        'w_o': nrm(ks[18], (DEPTH, D_MODEL, D_MODEL), D_MODEL ** -0.5),
        'norm_ffn': 1.0 + nrm(ks[19], (DEPTH, D_MODEL), 0.05),
        'w_gate_d': nrm(ks[20], (N_DENSE, D_MODEL, D_FF), D_MODEL ** -0.5),
        'w_up_d': nrm(ks[21], (N_DENSE, D_MODEL, D_FF), D_MODEL ** -0.5),
        'w_down_d': nrm(ks[22], (N_DENSE, D_FF, D_MODEL), D_FF ** -0.5),
        'w_router': nrm(ks[23], (N_MOE, D_MODEL, N_EXPERTS), D_MODEL ** -0.5),
        'b_router': nrm(ks[24], (N_MOE, N_EXPERTS), 0.01),
        'w_gate_e': nrm(ks[25], (N_MOE, N_EXPERTS, D_MODEL, D_FF_EXPERT), D_MODEL ** -0.5),
        'w_up_e': nrm(ks[26], (N_MOE, N_EXPERTS, D_MODEL, D_FF_EXPERT), D_MODEL ** -0.5),
        'w_down_e': nrm(ks[27], (N_MOE, N_EXPERTS, D_FF_EXPERT, D_MODEL), D_FF_EXPERT ** -0.5),
        'norm_final': 1.0 + nrm(ks[28], (D_MODEL,), 0.05),
    }

def reference(x_prompt, x_sample, cache_k, cache_v, state_conv, state_pool,
              norm_mix, w_in, conv_w, w_conv_out, w_pool, pool_scale,
              lambda_q1, lambda_k1, lambda_q2, lambda_k2, subln_g, w_attn_out, w_o,
              norm_ffn, w_gate_d, w_up_d, w_down_d,
              w_router, b_router, w_gate_e, w_up_e, w_down_e, norm_final):
    B, T = x_prompt.shape[0], x_prompt.shape[1]
    DT = x_sample.shape[1]
    P = cache_k.shape[2]
    pos_p = jnp.arange(T)
    pos_s = P + jnp.arange(DT)
    zero_conv = jnp.zeros((B, CONV_K - 1, CONV_W), x_prompt.dtype)
    zero_pool = jnp.zeros((B, POOL_HIST, POOL_W), x_prompt.dtype)
    xp, xs = x_prompt, x_sample
    kp_l, vp_l, cp_l, pp_l = [], [], [], []
    ks_l, vs_l, cs_l, ps_l = [], [], [], []
    for l in range(DEPTH):
        mix_w = (norm_mix[l], w_in[l], conv_w[l], w_conv_out[l], w_pool[l], pool_scale[l],
                 lambda_q1[l], lambda_k1[l], lambda_q2[l], lambda_k2[l], subln_g[l],
                 w_attn_out[l], w_o[l])
        xp, cp, pp, kp, vp = token_mixer(xp, pos_p, zero_conv, zero_pool, None, None, l, *mix_w)
        xs, cs, ps, kss, vss = token_mixer(xs, pos_s, state_conv[l], state_pool[l],
                                           cache_k[l], cache_v[l], l, *mix_w)
        kp_l.append(kp); vp_l.append(vp); cp_l.append(cp); pp_l.append(pp)
        ks_l.append(kss); vs_l.append(vss); cs_l.append(cs); ps_l.append(ps)
        ffn_w = (norm_ffn[l], w_gate_d, w_up_d, w_down_d, w_router, b_router, w_gate_e, w_up_e, w_down_e)
        xp = channel_mixer(xp, l, *ffn_w)
        xs = channel_mixer(xs, l, *ffn_w)
    y_prompt = rmsnorm(xp, norm_final)
    y_sample = rmsnorm(xs, norm_final)
    k_prompt = jnp.stack(kp_l)
    v_prompt = jnp.stack(vp_l)
    conv_prompt = jnp.stack(cp_l)
    pool_prompt = jnp.stack(pp_l)
    k_sample = jnp.stack(ks_l)
    v_sample = jnp.stack(vs_l)
    conv_sample = jnp.stack(cs_l)
    pool_sample = jnp.stack(ps_l)
    return (y_prompt, y_sample, k_prompt, v_prompt, conv_prompt, pool_prompt, k_sample, v_sample, conv_sample, pool_sample)


_drawn_inputs = setup_inputs


def setup_inputs(seed=0):
    import zlib

    import numpy as np

    out = dict(_drawn_inputs(seed))
    spreads = {}
    factors = {'b_router': 2.992}
    for name, (base, spread) in spreads.items():
        noise = np.random.default_rng([zlib.crc32(name.encode()), seed]).standard_normal(out[name].shape)
        drawn = base * np.exp(spread * noise) if base else spread * noise
        out[name] = __import__('jax').numpy.asarray(drawn.astype(out[name].dtype))
    for name, factor in factors.items():
        out[name] = (out[name] * factor).astype(out[name].dtype)
    return out
```

```python
from contextlib import ExitStack, contextmanager
import math

import concourse.bass as bass
from concourse import mybir

P = 128
F32 = mybir.dt.float32
F32R = mybir.dt.float32r
I32 = mybir.dt.int32
ALU = mybir.AluOpType
ACT = mybir.ActivationFunctionType
AX = mybir.AxisListType.X

D = 1024
KD = D // P
TP, TS = 512, 32
T = TP + TS
HALF = T // 2
NTT = 5
DEPTH = 2
PAST = 128
HEADS = 4
CW = 512
NC4 = CW // P
HIST = 15
FE = 1408
NF = FE // P
NE = 8
CAP = 208
CAPT = (128, CAP - 128)
MAXR = -(-T // CAP)
EPS = 1e-6
SUB_EPS = 1e-5
SCALE = 0.125
NEG = -1.0e30
BIG = -3.0e38

C_X, C_B, C_C, C_U, C_Q, C_K, C_V, C_G = (0, 512, 1024, 1536, 2048, 2560, 3072, 3584)

K_COS, K_SIN, K_ID, K_ROT, K_TRI, K_IOTA = 0, 544, 1088, 1216, 1344, 1472
K_RC, K_RANK = K_IOTA + CAP, K_IOTA + CAP + 4 * HIST
K_N = K_RANK + NE

R_MIX, R_FFN, R_PS, R_CW, R_SUB = 0, 16, 32, 48, 72
R_N = 74

NSLOT = 4
AHEAD = 2


def lam_init(l):
    return 0.8 - 0.6 * math.exp(-0.3 * l)


class Tally:

    def __init__(self, base=0):
        self.base, self.off = base, 0

    def now(self):
        return self.base + self.off

    def next(self, k=1):
        self.off += k
        return self.now()


class Tallies:

    def __init__(self, eng):
        self.eng, self.all = eng, {}

    def __getattr__(self, name):
        return self.all.setdefault(name, Tally())

    def of(self, name, i):
        return self.all.setdefault(f"{name}{i}", Tally())

    @contextmanager
    def trips(self, n, **per):
        for k in per:
            self.all.setdefault(k, Tally())
        saved = {k: (t.base, t.off) for k, t in self.all.items()}
        with self.eng.Fori(0, n) as i:
            for k, t in self.all.items():
                if per.get(k, 0):
                    t.base = t.base + t.off + i * per[k]
                    t.off = 0
            yield i
            got = {k: t.off - (0 if per.get(k, 0) else saved.get(k, (0, 0))[1]) for k, t in self.all.items()}
            bad = {k: (v, per.get(k, 0)) for k, v in got.items() if v != per.get(k, 0)}
            assert not bad, bad
        for k, t in self.all.items():
            b, o = saved.get(k, (0, 0))
            t.base, t.off = b, o + (n * per.get(k, 0) if isinstance(n, int) else 0)


def turns(jobs, times=1):
    return {f"slot{s}": times * len(range(s, jobs, NSLOT)) for s in range(NSLOT)}


def both(*parts):
    out = {}
    for p in parts:
        for k, v in p.items():
            out[k] = out.get(k, 0) + v
    return out


HEAD_J = [8] * 6
POOL_J = [8, 8, 8, 8]
GATE_J = [8, 8, 4, 1, 8, 4] * 2
OUT_J = [8, 8]
UP_J = [8, 8]
DOWN_J = [8, 8, NF - 8, NF - 8]
EXPERT_J = [8] * (2 * NF) + DOWN_J * 4


def program(nc, x_prompt, x_sample, cache_k, cache_v, state_conv, state_pool, norm_mix, w_in, conv_w, w_conv_out,
            w_pool, pool_scale, lambda_q1, lambda_k1, lambda_q2, lambda_k2, subln_g, w_attn_out, w_o, norm_ffn,
            w_gate_d, w_up_d, w_down_d, w_router, b_router, w_gate_e, w_up_e, w_down_e, norm_final, consts,
            y_prompt, y_sample, k_prompt, v_prompt, conv_prompt, pool_prompt, k_sample, v_sample, conv_sample,
            pool_sample):
    ctx = ExitStack()

    def sb(name, shape, dt=F32):
        return ctx.enter_context(nc.sbuf_tensor(name, shape, dt))

    def sem(name):
        return ctx.enter_context(nc.semaphore(name))

    raw = sb("raw", [P, NSLOT, 1024])
    whi = sb("whi", [P, NSLOT, 1024], F32R)
    wlo = sb("wlo", [P, NSLOT, 1024], F32R)
    hhi = sb("hhi", [P, KD, T], F32R)
    hlo = sb("hlo", [P, KD, T], F32R)
    bhi = sb("bhi", [P, 12, T], F32R)
    blo = sb("blo", [P, 12, T], F32R)
    with nc.sbuf_tensor("conv_work", [P, 3 * T + 6], F32) as conv_work:
        pass
    selr = sb("selr", [P, NTT * CAP + 2 * T], F32R)
    xT = sb("xT", [P, KD, T])
    arena = sb("arena", [P, 9664])
    kc = sb("kc", [P, K_N])
    par = sb("par", [P, R_N])
    ones = sb("ones", [P, P])
    stT = sb("stT", [P, NC4, 34])
    tails = sb("tails", [P, NC4, 34])
    small = sb("small", [P, 64])
    rounds_i = sb("rounds_i", [P, 2], I32)
    ps = ctx.enter_context(nc.psum_tensor("ps", [P, 8, 512], F32))

    def ar(at, n, rows=P):
        return arena[0:rows, at:at + n]

    ident = kc[:, K_ID:K_ID + P]
    neglam = small[:, 0:2]
    smax = small[:, 2:4]
    nbias = small[:, 4:6]
    psum2 = small[:, 6:8]
    prcp = small[:, 8:10]
    osum = small[:, 10:30]
    orms = small[:, 30:50]
    lam4 = small[:, 50:54]
    fsum = small[:, 54:59]
    frms = small[:, 59:64]

    landed = [sem(f"landed{s}") for s in range(NSLOT)]
    hi_ready = [sem(f"hi_ready{s}") for s in range(NSLOT)]
    lo_ready = [sem(f"lo_ready{s}") for s in range(NSLOT)]
    used = [sem(f"used{s}") for s in range(NSLOT)]
    free = [sem(f"result_free{p}") for p in range(4)]
    s_const, s_x, s_rows, s_lam, s_state = (sem(n) for n in ("const_in", "x_in", "rows_in", "lambda_in", "state_in"))
    s_cache = sem("cache_in")
    s_ones = sem("ones_set")
    s_pace = sem("pace")
    s_turned = sem("input_turned")
    s_kept = sem("input_kept")
    s_lamp = sem("lambda_products")
    s_lame = sem("lambda_exp")
    s_dve = sem("dve_step")
    s_act = sem("act_step")
    s_sq = sem("squares")
    s_sum = sem("squares_summed")
    s_ms = sem("mean_square")
    s_rms = sem("root_mean_square")
    s_hf = sem("h_full")
    s_hh = sem("h_hi")
    s_hl = sem("h_lo")
    s_rot = sem("rotated")
    s_rope = sem("rope_done")
    s_vt = sem("v_turned")
    s_vtok = sem("v_tokens")
    s_kt = sem("k_turned")
    s_ktok = sem("k_tokens")
    s_kv = sem("kv_stored")
    s_sc = sem("scores")
    s_mx = sem("score_max")
    s_exp = sem("probabilities")
    s_a = sem("difference")
    s_at = sem("difference_turned")
    s_ak = sem("difference_kept")
    s_pv = sem("attended")
    s_ok = sem("attended_kept")
    s_osq = sem("attended_squares")
    s_on = sem("attended_normed")
    s_ot = sem("attended_turned")
    s_oh = sem("attended_hi")
    s_ol = sem("attended_lo")
    s_by = sem("branch_full")
    s_bh = sem("branch_hi")
    s_bl = sem("branch_lo")
    s_pad = sem("pool_pads")
    s_tt = sem("tails_turned")
    s_tk = sem("tails_kept")
    s_ts = sem("tails_stored")
    s_mg = sem("merged")
    s_mh = sem("merged_hi")
    s_ml = sem("merged_lo")
    s_xr = sem("residual_ready")
    s_fh = sem("hidden_hi")
    s_fl = sem("hidden_lo")
    s_wr = sem("router_in")
    s_rw = sem("router_split")
    s_lg = sem("logits")
    s_rt = sem("routes")
    s_re = sem("route_exp_in")
    s_rx = sem("route_exp")
    s_pos = sem("positions")
    s_go = sem("rounds_known")
    s_ht = sem("rows_turned")
    s_hk = sem("rows_kept_act")
    s_hkd = sem("rows_kept_dve")
    s_sel = sem("selection")
    s_ga = sem("gathered")
    s_gh = sem("gathered_hi")
    s_gl = sem("gathered_lo")
    s_st = sem("selection_turned")
    s_stk = sem("selection_turned_kept")
    s_yd = sem("expert_out_kept")
    s_yt = sem("expert_out_turned")
    s_yh = sem("expert_out_hi")
    s_yl = sem("expert_out_lo")
    s_sp = sem("spread")
    s_acc = sem("spread_added")
    s_mix = sem("experts_added")
    s_fsq = sem("final_squares")
    s_frm = sem("final_root")
    s_fin = sem("final_rows")
    s_gf = sem("final_gain_in")
    s_out = sem("outputs_stored")

    block = ctx.enter_context(nc.Block())

    XIN = 0
    ROWS = 5120
    STROWS = ROWS + P
    LAMB = STROWS + 512
    QR, KR, VR, TMP, QT, KT = 0, 544, 1088, 1632, 2176, 2720
    VTOK, KTOK, PROB, AT, OQ, KPT, VP = 3264, 3904, 4544, 5568, 6080, 8640, 9152
    SQ, MS, HF = 0, 5120, 7104
    UX, PA, PB, PM = 2224, 3376, 3952, 0
    TROW = 6528
    M, SA, SB_, SC_, GT = 0, 4352, 4896, 5440, 5984
    FS, FA = 4352, 4896
    XTOK, YT = 0, NTT * D
    ES = YT + KD * CAP
    EA = ES + 2 * CAP
    RT = EA + 2 * CAP
    GF = YT

    xs, ext, cv = (conv_work[:, a:a + n] for a, n in ((0, T), (T, T + 4), (2 * T + 4, T + 2)))
    oq = ar(OQ, NTT * HEADS * P).rearrange("p (b h e) -> p b h e", b=NTT, h=HEADS)
    prob = ar(PROB, 1024).rearrange("p (c n) -> p c n", c=2)
    vtok = ar(VTOK, NTT * P).rearrange("p (j e) -> p j e", j=NTT)
    ktok = ar(KTOK, NTT * P).rearrange("p (j e) -> p j e", j=NTT)
    kpT = ar(KPT, 512).rearrange("p (h t) -> p h t", h=HEADS)
    vpast = ar(VP, 512).rearrange("p (h e) -> p h e", h=HEADS)
    mrg = ar(M, KD * T).rearrange("p (k t) -> p k t", k=KD)
    xtok = ar(XTOK, NTT * D).rearrange("p (j d) -> p j d", j=NTT)
    yT = ar(YT, KD * CAP).rearrange("p (k c) -> p k c", k=KD)

    bflat_hi, bflat_lo = (t[:, :, :].rearrange("p k t -> p (k t)") for t in (bhi, blo))
    hflat_hi, hflat_lo = (t[:, :, :].rearrange("p k t -> p (k t)") for t in (hhi, hlo))
    htok = [f[:, 0:NTT * D].rearrange("p (j d) -> p j d", j=NTT) for f in (bflat_hi, bflat_lo)]
    hg = [f[:, NF * CAP:(NF + KD) * CAP].rearrange("p (k c) -> p k c", k=KD) for f in (hflat_hi, hflat_lo)]
    ea = [f[:, 0:NF * CAP].rearrange("p (k c) -> p k c", k=NF) for f in (hflat_hi, hflat_lo)]
    ey = [f[:, 0:2 * D].rearrange("p (a d) -> p a d", a=2) for f in (hflat_hi, hflat_lo)]
    sel = selr[:, 0:NTT * CAP].rearrange("p (j c) -> p j c", j=NTT)
    selT = selr[:, NTT * CAP:].rearrange("p (a t) -> p a t", a=2)
    def rt(i):
        return ar(RT + 40 * i, 40).rearrange("p (j e) -> p j e", j=NTT)
    LG, EQ, OH1, OH2, RM, WT, PS_, T1, T2, SL = (rt(i) for i in range(10))
    R1 = ar(RT + 400, 5), ar(RT + 405, 5), ar(RT + 410, 5), ar(RT + 415, 5), ar(RT + 420, 5)
    rcnt = ar(RT + 425, 8)
    rmaxc = ar(RT + 433, 1)
    rnd = ar(RT + 434, 1)
    rtmp = ar(RT + 435, 3)
    BR = ar(RT + 440, 8)
    WR = ar(RT + 448, 64).rearrange("p (k e) -> p k e", k=KD)

    def bank2(p):
        return ps[:, 2 * p:2 * p + 2, 0:HALF]

    def halves(ap):
        return ap.rearrange("p (a n) -> p a n", a=2)

    def kview(w):
        return w.rearrange("(k p) n -> p k n", p=P)

    def units():
        for b in range(4):
            yield b, P, b * P, (b + 1) * P, [P] * (b + 1)
        yield 4, TS, TP, PAST + TS, [PAST, TS]

    @block.sync
    def _(sp):
        c = Tallies(sp)
        pos = [0]

        def load(src, kt, alone=False):
            s = pos[0] % NSLOT
            pos[0] += 1
            n = c.of("slot", s).next()
            sp.wait_ge(lo_ready[s], n)
            if alone:
                sp.sem_inc(s_pace, 1)
            sp.dma_start(raw[:, s, 0:kt * P].rearrange("p (k n) -> p k n", k=kt), src).then_inc(landed[s], 16)

        sp.dma_start(kc[:], consts).then_inc(s_const, 16)
        sp.dma_start(ar(XIN, 4096).rearrange("p (j d) -> p j d", j=4),
                     x_prompt[0].rearrange("(j p) d -> p j d", p=P)).then_inc(s_x, 16)
        sp.dma_start(ar(XIN + 4096, D, TS), x_sample[0]).then_inc(s_x, 16)

        for l in range(DEPTH):
            w = w_in[l]
            with c.trips(HEADS, **turns(6)) as h:
                pos[0] = 0
                for col in (C_Q, C_K, C_V, C_X, C_C, C_B):
                    load(kview(w[:, bass.ds(h * P + col, P)]), 8, True)
            pos[0] = 0
            for g in range(4):
                load(kview(w[:, C_U + g * P:C_U + (g + 1) * P]), 8)
            with c.trips(4, **turns(12)) as g:
                pos[0] = 0
                for d2 in range(2):
                    at = g * 256 + d2 * P
                    load(kview(w[:, bass.ds(at + C_G, P)]), 8)
                    load(kview(w[:, bass.ds(at + (C_G + D), P)]), 8)
                    load(kview(w_conv_out[l][:, bass.ds(at, P)]), 4, True)
                    load(kview(w_pool[l, bass.ds(g, 1), :, d2 * P:(d2 + 1) * P].rearrange("a c n -> (a c) n")), 1)
                    load(kview(w[:, bass.ds(at + (C_G + 2 * D), P)]), 8)
                    load(kview(w_attn_out[l][:, bass.ds(at, P)]), 4)
            with c.trips(4, **turns(2)) as m2:
                pos[0] = 0
                for j in range(2):
                    load(kview(w_o[l][:, bass.ds(m2 * 256 + j * P, P)]), 8)
            if l == 0:
                with c.trips(2, **both(turns(2, NF), turns(4, 4))) as ch:
                    with c.trips(NF, **turns(2)) as f:
                        pos[0] = 0
                        at = ch * FE + f * P
                        load(kview(w_gate_d[0][:, bass.ds(at, P)]), 8)
                        load(kview(w_up_d[0][:, bass.ds(at, P)]), 8)
                    with c.trips(4, **turns(4)) as m2:
                        pos[0] = 0
                        for k0, k1 in ((0, 8), (8, NF)):
                            for j in range(2):
                                load(kview(w_down_d[0][bass.ds(ch * FE + k0 * P, (k1 - k0) * P),
                                                       bass.ds(m2 * 256 + j * P, P)]), k1 - k0)
            else:
                def expert_tile(j, e):
                    e1 = bass.ds(e, 1) if not isinstance(e, int) else slice(e, e + 1)
                    if j < 2 * NF:
                        w, rs, n0 = (w_gate_e, w_up_e)[j % 2], slice(0, D), j // 2
                    else:
                        m2, q = divmod(j - 2 * NF, 4)
                        w, rs, n0 = w_down_e, (slice(0, D), slice(D, FE))[q // 2], 2 * m2 + q % 2
                    return kview(w[0, e1, rs, n0 * P:(n0 + 1) * P].rearrange("a d n -> (a d) n")), EXPERT_J[j]

                pos[0] = 0
                for j in range(AHEAD):
                    load(*expert_tile(j, 0))
                sp.wait_ge(s_go, 1)
                rounds = sp.value_load(rounds_i[0:1, 0:1], min_val=1, max_val=MAXR)
                per = turns(len(EXPERT_J))
                with c.trips(rounds, **{k: NE * v for k, v in per.items()}) as r:
                    with c.trips(NE, **per) as e:
                        pos[0] = AHEAD
                        for j in range(AHEAD, len(EXPERT_J)):
                            load(*expert_tile(j, e), j >= 2 * NF)
                        pos[0] = 0
                        for j in range(AHEAD):
                            load(*expert_tile(j, (e + 1) % NE), True)

    @block.gpsimd
    def _(pool):
        c = Tallies(pool)
        for dst, src in ((R_MIX, norm_mix.rearrange("l (k p) -> (l k) p", p=P)),
                         (R_FFN, norm_ffn.rearrange("l (k p) -> (l k) p", p=P)),
                         (R_PS, pool_scale.rearrange("l (k p) -> (l k) p", p=P)),
                         (R_CW, conv_w.rearrange("l j (k p) -> (l j k) p", p=P)),
                         (R_SUB, subln_g)):
            pool.dma_start(arena[dst:dst + src.shape[0], ROWS:ROWS + P], src).then_inc(s_rows, 16)
        for l in range(DEPTH):
            pool.dma_start(arena[17 * l:17 * l + 2, STROWS:STROWS + 512], state_conv[l, 0]).then_inc(s_state, 16)
            pool.dma_start(arena[17 * l + 2:17 * l + 17, STROWS:STROWS + 512], state_pool[l, 0]).then_inc(s_state, 16)
        for i, a in enumerate((lambda_q1, lambda_k1, lambda_q2, lambda_k2)):
            pool.dma_start(ar(LAMB + P * i, P),
                           a.rearrange("(a l) d -> a (l d)", a=1).partition_broadcast(P)
                           .rearrange("p a n -> p (a n)")).then_inc(s_lam, 16)
        for l in range(DEPTH):
            if l == 0:
                pool.wait_ge(s_kept, KD)
            else:
                pool.wait_ge(s_xr, 2 * l)
            pool.dma_start(ar(PROB, 512), cache_k[l, 0].rearrange("t h e -> t (h e)")).then_inc(s_cache, 16)
            pool.dma_start(ar(VP, 512), cache_v[l, 0].rearrange("t h e -> t (h e)")).then_inc(s_cache, 16)
            with c.trips(HEADS, vtok=1, ktok=1) as h:
                h1 = bass.ds(h, 1)
                pool.wait_ge(s_vtok, c.vtok.next() + 1)
                pool.sem_inc(s_pace, 1)
                pool.dma_start(v_prompt[l, 0, :, h1, :].rearrange("(j p) h e -> p j (h e)", p=P),
                               vtok[:, 0:4, :]).then_inc(s_kv, 16)
                pool.dma_start(v_sample[l, 0, :, h1, :].rearrange("t h e -> t (h e)"),
                               vtok[0:TS, 4, :]).then_inc(s_kv, 16)
                pool.wait_ge(s_ktok, c.ktok.next())
                pool.sem_inc(s_pace, 1)
                pool.dma_start(k_prompt[l, 0, :, h1, :].rearrange("(j p) h e -> p j (h e)", p=P),
                               ktok[:, 0:4, :]).then_inc(s_kv, 16)
                pool.dma_start(k_sample[l, 0, :, h1, :].rearrange("t h e -> t (h e)"),
                               ktok[0:TS, 4, :]).then_inc(s_kv, 16)
            pool.wait_ge(s_tk, l + 1)
            for dst, a, b in ((conv_prompt, 0, 2), (conv_sample, 2, 4), (pool_prompt, 4, 19), (pool_sample, 19, 34)):
                pool.dma_start(dst[l, 0], arena[a:b, TROW:TROW + 512]).then_inc(s_ts, 16)
        pool.wait_ge(s_hl, 4 * KD)
        pool.dma_start(WR, kview(w_router[0])).then_inc(s_wr, 16)
        pool.dma_start(BR, b_router.partition_broadcast(P).rearrange("p a n -> p (a n)")).then_inc(s_wr, 16)
        pool.wait_ge(s_mix, 1)
        pool.dma_start(ar(GF, D), norm_final.rearrange("(a n) -> a n", a=1).partition_broadcast(P)
                       .rearrange("p a n -> p (a n)")).then_inc(s_gf, 16)
        for j in range(NTT):
            pool.wait_ge(s_fin, j + 1)
            if j < 4:
                pool.dma_start(y_prompt[0, j * P:(j + 1) * P, :], xtok[:, j, :]).then_inc(s_out, 16)
            else:
                pool.dma_start(y_sample[0], xtok[0:TS, 4, :]).then_inc(s_out, 16)
        pool.wait_ge(s_out, 16 * NTT)
        pool.wait_ge(s_kv, 64 * HEADS * DEPTH)
        pool.wait_ge(s_ts, 64 * DEPTH)

    @block.tensor
    def _(pe):
        c = Tallies(pe)
        pos = [0]
        for s in range(NSLOT):
            pe.sem_inc(used[s], 1)
        for p in range(4):
            pe.sem_inc(free[p], 1)

        def product(kt, k0, act_hi, act_lo, p, start=True, stop=True, made=None):
            s = pos[0] % NSLOT
            pos[0] += 1
            if start:
                pe.wait_ge(free[p], c.of("pair", p).next())
            pe.wait_ge(lo_ready[s], c.of("slot", s).next() + 1)
            for k in range(kt):
                if made:
                    pe.wait_ge(made[0], made[1] + k + 1)
                ks = slice(k * P, (k + 1) * P)
                for i, (w, a) in enumerate(((whi, act_hi), (whi, act_lo), (wlo, act_hi))):
                    for q in range(2):
                        mm = pe.matmul(ps[:, 2 * p + q, 0:HALF], w[:, s, ks], a(k0 + k)[:, q * HALF:(q + 1) * HALF],
                                       start=(start and k == 0 and i == 0), stop=(stop and k == kt - 1 and i == 2))
            mm.then_inc(used[s], 1)

        def part(j, p, k0, k1):
            s = j % NSLOT
            if k0 == 0:
                pe.wait_ge(free[p], c.of("pair", p).next())
                pe.wait_ge(lo_ready[s], c.of("slot", s).next() + 1)
            for k in range(k0, k1):
                ks = slice(k * P, (k + 1) * P)
                for i, (w, a) in enumerate(((whi, hhi), (whi, hlo), (wlo, hhi))):
                    for q in range(2):
                        mm = pe.matmul(ps[:, 2 * p + q, 0:HALF], w[:, s, ks], a[:, k, q * HALF:(q + 1) * HALF],
                                       start=(k == 0 and i == 0), stop=(k == KD - 1 and i == 2))
            if k1 == KD:
                mm.then_inc(used[s], 1)

        def rows(t, at=0):
            return lambda k: t[:, at + k, :]

        def norm_sums():
            for k in range(KD):
                pe.wait_ge(s_sq, c.sq.next())
                for q in range(2):
                    mm = pe.matmul(ps[:, 4 + q, 0:HALF], ones[:], ar(SQ + T * k + q * HALF, HALF),
                                   start=(k == 0), stop=(k == KD - 1))
                mm.then_inc(s_sum, 1)

        pe.wait_ge(s_const, 16)
        pe.wait_ge(s_x, 32)
        for k in range(KD):
            if k >= 4:
                pe.wait_ge(s_kept, k - 3)
            b = 2 * (k % 4)
            for j in range(NTT):
                n = P if j < 4 else TS
                mm = pe.transpose(ps[:, b + j // 4, (j % 4) * P:(j % 4) * P + n],
                                  ar(XIN + j * D + k * P, P, n), ident[0:n, 0:n])
            mm.then_inc(s_turned, 1)
        pe.wait_ge(s_rows, 80)
        pe.wait_ge(s_kept, KD)
        pe.transpose(ps[:, 0, 0:R_N], ar(ROWS, P, R_N), ident[0:R_N, 0:R_N]).then_inc(s_turned, 1)
        pe.wait_ge(s_state, 64)
        for t in range(NC4):
            mm = pe.transpose(ps[:, 1, t * P:t * P + 34], ar(STROWS + t * P, P, 34), ident[0:34, 0:34])
        mm.then_inc(s_turned, 1)
        pe.wait_ge(s_kept, KD + 2)
        pe.wait_ge(s_ones, 1)

        for l in range(DEPTH):
            norm_sums()
            pe.wait_ge(s_cache, 32 * (l + 1))
            for h in range(HEADS):
                mm = pe.transpose(ps[:, 6, h * P:(h + 1) * P], ar(PROB + h * P, P), ident)
            mm.then_inc(s_turned, 1)

            with c.trips(HEADS, **turns(6), pair0=3, pair1=3, rope=2, vtok=1, ktok=1, exp=5, a=5, ak=5, ok=5) as h:
                pos[0] = 0
                h1 = bass.ds(h, 1)
                for p in (0, 1, 0):
                    product(8, 0, rows(hhi), rows(hlo), p, made=(s_hl, 2 * l * KD) if pos[0] == 0 else None)
                pe.wait_ge(s_kept, KD + 3 + l)
                for q in range(2):
                    mm = pe.matmul(ps[:, 4 + q, 0:HALF], kc[:, K_ROT:K_ROT + P], ar(QR + q * HALF, HALF),
                                   start=True, stop=True)
                mm.then_inc(s_rot, 1)
                pe.wait_ge(free[1], c.of("pair", 1).now() + 1)
                pe.wait_ge(s_ok, c.ok.now() + 1)
                for q in range(2):
                    mm = pe.matmul(ps[:, 6 + q, 0:HALF], kc[:, K_ROT:K_ROT + P], ar(KR + q * HALF, HALF),
                                   start=True, stop=True)
                mm.then_inc(s_rot, 1)
                part(3, 1, 0, 2)
                pe.wait_ge(free[0], c.of("pair", 0).now() + 1)
                pe.wait_ge(s_rope, c.rope.next() + 1)
                for j in range(NTT):
                    n = P if j < 4 else TS
                    mm = pe.transpose(ps[0:n, 4 + j // 4, (j % 4) * P:(j % 4 + 1) * P], ar(VR + j * P, n), ident)
                mm.then_inc(s_vt, 1)
                part(3, 1, 2, 4)
                pe.wait_ge(s_rope, c.rope.next() + 1)
                for j in range(NTT):
                    n = P if j < 4 else TS
                    mm = pe.transpose(ps[0:n, 6 + j // 4, (j % 4) * P:(j % 4 + 1) * P], ar(KT + j * P, n), ident)
                mm.then_inc(s_kt, 1)
                pe.wait_ge(s_vtok, c.vtok.next() + 1)

                def scores(u, rq, q0, keys, tiles):
                    if u:
                        pe.wait_ge(s_exp, c.exp.next())
                        pe.sem_inc(s_pace, 1)
                    for cc in range(2):
                        r = slice(64 * cc, 64 * cc + 64)
                        qs = arena[r, QT + q0:QT + q0 + rq]
                        if u < 4:
                            mm = pe.matmul(ps[0:rq, 4 + cc, 0:keys], qs, arena[r, KT:KT + keys], start=True, stop=True)
                        else:
                            pe.matmul(ps[0:rq, 4 + cc, 0:PAST], qs, arena[r, TMP:TMP + PAST], start=True, stop=True)
                            mm = pe.matmul(ps[0:rq, 4 + cc, PAST:keys], qs, arena[r, KT + TP:KT + T],
                                           start=True, stop=True)
                    mm.then_inc(s_sc, 1)

                us = list(units())
                scores(*us[0])
                part(3, 1, 4, 8)
                pe.wait_ge(s_ktok, c.ktok.next())
                for u, rq, q0, keys, tiles in us:
                    if u < 4:
                        scores(*us[u + 1])
                    else:
                        part(5, 1, 6, 8)
                    pe.wait_ge(s_a, c.a.next())
                    pe.sem_inc(s_pace, 1)
                    for j, kn in enumerate(tiles):
                        mm = pe.transpose(ps[0:kn, 6, j * P:j * P + rq], prob[0:rq, 0, j * P:j * P + kn],
                                          ident[0:rq, 0:rq])
                    mm.then_inc(s_at, 1)
                    if u < 4:
                        part(*((4, 0, 0, 4), (4, 0, 4, 8), (5, 1, 0, 4), (5, 1, 4, 6))[u])
                    pe.wait_ge(s_ok, c.ok.next())
                    pe.wait_ge(s_ak, c.ak.next())
                    for j, kn in enumerate(tiles):
                        if u < 4:
                            v = vtok[:, j, :]
                        else:
                            v = vpast[:, h1, :].rearrange("p h e -> p (h e)") if j == 0 else vtok[0:TS, 4, :]
                        mm = pe.matmul(ps[0:rq, 7, 0:P], ar(AT + j * P, rq, kn), v,
                                       start=(j == 0), stop=(j == len(tiles) - 1))
                    mm.then_inc(s_pv, 1)
                c.exp.next()

            pos[0] = 0
            for g in range(4):
                product(8, 0, rows(hhi), rows(hlo), g % 2)
                if g % 2 == 0:
                    continue
                pe.wait_ge(s_on, l + 1)
                pe.wait_ge(s_ok, c.ok.now() + 1)
                for h in (g - 1, g):
                    if h >= 2:
                        pe.wait_ge(s_ol, 4 * l + h - 1)
                    b = 4 + 2 * (h % 2)
                    for j in range(NTT):
                        n = P if j < 4 else TS
                        mm = pe.transpose(ps[:, b + j // 4, (j % 4) * P:(j % 4) * P + n], oq[0:n, j, h, :],
                                          ident[0:n, 0:n])
                    mm.then_inc(s_ot, 1)

            with c.trips(4, **turns(12), pair0=6, pair1=6) as g:
                pos[0] = 0
                g4 = bass.ds(g + 4, 1)
                for d2 in range(2):
                    product(8, 0, rows(hhi), rows(hlo), 0)
                    product(8, 0, rows(hhi), rows(hlo), 1)
                    pe.wait_ge(s_bl, 8 * l + 4 + 1)
                    product(4, 0, rows(bhi), rows(blo), 0)
                    pe.wait_ge(s_bl, 8 * l + 8 + 1)
                    product(1, 0, lambda k: bhi[:, g4, :].rearrange("p a t -> p (a t)"),
                            lambda k: blo[:, g4, :].rearrange("p a t -> p (a t)"), 1)
                    product(8, 0, rows(hhi), rows(hlo), 0)
                    pe.wait_ge(s_ol, 4 * l + 4)
                    product(4, 0, rows(bhi, 8), rows(blo, 8), 1)

            for t in range(NC4):
                mm = pe.transpose(ps[0:34, 6, t * P:(t + 1) * P], tails[:, t, :], ident)
            mm.then_inc(s_tt, 1)
            with c.trips(4, **turns(2), pair0=1, pair1=1):
                pos[0] = 0
                for j in range(2):
                    product(8, 0, rows(bhi), rows(blo), j, made=(s_ml, l * KD) if j == 0 else None)
            norm_sums()
            if l:
                pe.wait_ge(s_hl, (2 * l + 2) * KD)
            if l == 0:
                with c.trips(2, **both(turns(2, NF), turns(4, 4)), pair0=NF + 4, pair1=NF + 4, fl=NF):
                    with c.trips(NF, **turns(2), pair0=1, pair1=1):
                        pos[0] = 0
                        product(8, 0, rows(hhi), rows(hlo), 0, made=(s_hl, KD))
                        product(8, 0, rows(hhi), rows(hlo), 1)
                    with c.trips(4, **turns(4), pair0=1, pair1=1):
                        pos[0] = 0
                        for k0, k1 in ((0, 8), (8, NF)):
                            pe.wait_ge(s_fl, c.fl.now() + k1)
                            pe.sem_inc(s_pace, 1)
                            for j in range(2):
                                product(k1 - k0, k0, rows(bhi), rows(blo), j, k0 == 0, k1 == NF)
                    c.fl.next(NF)

        pe.wait_ge(s_rw, 2)
        for j in range(NTT):
            n = P if j < 4 else TS
            for k in range(KD):
                for i, (a, w) in enumerate(((hhi, 0), (hlo, 0), (hhi, 1))):
                    mm = pe.matmul(ps[0:n, 0, 8 * j:8 * j + 8], a[:, k, j * P:j * P + n],
                                   selr[:, w * 64 + k * 8:w * 64 + k * 8 + 8],
                                   start=(k == 0 and i == 0), stop=(k == KD - 1 and i == 2))
        mm.then_inc(s_lg, 1)
        n_t = 0
        for j in range(NTT):
            n = P if j < 4 else TS
            for src in (hhi, hlo, xT):
                for g in range(2):
                    b = 2 + n_t % 4
                    if n_t >= 4:
                        pe.wait_ge(s_hk, sum(1 for i in range(n_t - 3) if i % 6 < 4))
                        if any(i % 6 >= 4 for i in range(n_t - 3)):
                            pe.wait_ge(s_hkd, sum(1 for i in range(n_t - 3) if i % 6 >= 4))
                    for k in range(4):
                        v = src[:, 4 * g + k, j * P:j * P + n]
                        if src is not xT:
                            v = v.bitcast(F32)
                        mm = pe.transpose(ps[0:n, b, k * P:(k + 1) * P], v, ident)
                    mm.then_inc(s_ht, 1)
                    n_t += 1
        pe.wait_ge(s_rt, 1)
        for j in range(NTT):
            n = P if j < 4 else TS
            for i in range(j + 1):
                kn = P if i < 4 else TS
                mm = pe.matmul(ps[0:n, 6, 8 * j:8 * j + 8], (kc[0:kn, K_TRI:K_TRI + n] if i == j else ones[0:kn, 0:n]),
                               RM[0:kn, i, :], start=(i == 0), stop=(i == j))
        for i in range(NTT):
            kn = P if i < 4 else TS
            mm = pe.matmul(ps[:, 7, 0:8], ones[0:kn, :], RM[0:kn, i, :], start=(i == 0), stop=(i == NTT - 1))
        mm.then_inc(s_pos, 1)
        pe.wait_ge(s_hk, 20)
        pe.wait_ge(s_hkd, 10)
        pe.wait_ge(s_go, 1)
        rounds = pe.value_load(rounds_i[0:1, 0:1], min_val=1, max_val=MAXR)
        per = both(turns(len(EXPERT_J)), dict(pair0=6 + 4, pair1=6 + 4, pair2=5, pair3=5, sel=1, gl=8, stk=1,
                                              fl=NF, yd=8, yl=2, acc=10))

        def product_e(kt, k0, a, b, start=True, stop=True):
            s = pos[0] % NSLOT
            pos[0] += 1
            if start:
                pe.wait_ge(free[b], c.of("pair", b).next())
            pe.wait_ge(lo_ready[s], c.of("slot", s).next() + 1)
            for k in range(kt):
                ks = slice(k * P, (k + 1) * P)
                for i, (w, v) in enumerate(((whi, a[0]), (whi, a[1]), (wlo, a[0]))):
                    mm = pe.matmul(ps[:, b, 0:CAP], w[:, s, ks], v[:, k0 + k, :],
                                   start=(start and k == 0 and i == 0), stop=(stop and k == kt - 1 and i == 2))
            mm.then_inc(used[s], 1)

        with c.trips(rounds, **{k: NE * v for k, v in per.items()}):
            with c.trips(NE, **per):
                pos[0] = 0
                pe.wait_ge(s_sel, c.sel.next())
                for d in range(KD):
                    if d == 0:
                        pe.wait_ge(s_acc, c.acc.now() + 4)
                    if d >= 4:
                        pe.wait_ge(s_gl, c.gl.now() + d - 3)
                    for j in range(NTT):
                        kn = P if j < 4 else TS
                        for i in range(2):
                            mm = pe.matmul(ps[:, 4 + d % 4, 0:CAP], htok[i][0:kn, j, d * P:(d + 1) * P],
                                           sel[0:kn, j, :], start=(j == 0 and i == 0), stop=(j == NTT - 1 and i == 1))
                    mm.then_inc(s_ga, 1)
                for a, cn in enumerate(CAPT):
                    pe.wait_ge(s_gl, c.gl.now() + (6 if a == 0 else 8))
                    pe.sem_inc(s_pace, 1)
                    for j in range(NTT):
                        kn = P if j < 4 else TS
                        mm = pe.transpose(ps[0:cn, 4 + 2 * a + j // 4, (j % 4) * P:(j % 4) * P + kn],
                                          sel[0:kn, j, a * P:a * P + cn].bitcast(F32), ident[0:kn, 0:kn])
                mm.then_inc(s_st, 1)
                c.gl.next(8)
                for f in range(NF):
                    product_e(8, 0, hg, 2 * (f % 2))
                    product_e(8, 0, hg, 2 * (f % 2) + 1)
                for m2 in range(4):
                    for k0, k1 in ((0, 8), (8, NF)):
                        if m2 == 0:
                            pe.wait_ge(s_fl, c.fl.now() + k1)
                            pe.sem_inc(s_pace, 1)
                        for j in range(2):
                            product_e(k1 - k0, k0, ea, j, k0 == 0, k1 == NF)
                c.fl.next(NF)
                pe.wait_ge(s_yd, c.yd.next(8))
                pe.wait_ge(s_stk, c.stk.next())
                pe.sem_inc(s_pace, 1)
                for a, cn in enumerate(CAPT):
                    for k in range(KD):
                        mm = pe.transpose(ps[0:cn, 4 + 2 * a + k // 4, (k % 4) * P:(k % 4 + 1) * P],
                                          yT[:, k, a * P:a * P + cn], ident)
                    mm.then_inc(s_yt, 1)
                pe.wait_ge(s_yl, c.yl.next(2))
                for n in range(2 * NTT):
                    j, g = n // 2, n % 2
                    rows_ = P if j < 4 else TS
                    if n >= 4:
                        pe.wait_ge(s_acc, c.acc.now() + 4 + n - 3)
                    for a, cn in enumerate(CAPT):
                        for i in range(2):
                            mm = pe.matmul(ps[0:rows_, 4 + n % 4, 0:512], selT[0:cn, a, j * P:j * P + rows_],
                                           ey[i][0:cn, a, g * 512:(g + 1) * 512],
                                           start=(a == 0 and i == 0), stop=(a == 1 and i == 1))
                    mm.then_inc(s_sp, 1)
                c.acc.next(10)

    @block.scalar
    def _(act):
        c = Tallies(act)
        pos = [0]

        def split(js, p):
            kt = js[p] if p < len(js) else 8
            s = (p if p < len(js) else p - len(js)) % NSLOT
            n = c.of("slot", s).next()
            act.wait_ge(landed[s], n * 16)
            act.wait_ge(used[s], n)
            act.activation(whi[:, s, 0:kt * P], raw[:, s, 0:kt * P], ACT.Copy).then_inc(hi_ready[s], 1)

        def ready(j):
            n = c.of("seen", j % NSLOT).next()
            act.wait_ge(used[j % NSLOT], n + 1)

        def skip(j):
            c.of("seen", j % NSLOT).next()

        def seen(n, times=1):
            return {k.replace("slot", "seen"): v for k, v in turns(n, times).items()}

        def norm_act(residual):
            for k in range(KD):
                if residual:
                    act.wait_ge(free[k % 2], c.of("pair", k % 2).now() - (3 - k // 2) + 1)
                act.activation(ar(SQ + T * k, T), xT[:, k, :], ACT.Square).then_inc(s_sq, 1)
            act.activation(small[0:1, 63:64], ones[0:1, 0:1], ACT.Sqrt)
            act.wait_ge(s_ms, c.ms.next())
            act.activation(ar(MS, T), ar(MS, T), ACT.Sqrt).then_inc(s_rms, 1)
            for k in range(KD):
                act.wait_ge(s_hf, c.hf.next())
                act.activation(hhi[:, k, :], ar(HF + T * (k % 2), T), ACT.Copy).then_inc(s_hh, 1)

        act.wait_ge(s_lamp, 1)
        act.activation(lam4, lam4, ACT.Exp).then_inc(s_lame, 1)
        for s in range(AHEAD):
            split([8, 8], s)
        act.wait_ge(s_kept, KD + 2)

        for l in range(DEPTH):
            norm_act(l > 0)
            with c.trips(HEADS, **turns(6), **seen(6), pair0=3, pair1=3, rope=2, vtok=1, mx=5, at=5, bl=1) as h:
                h1 = bass.ds(h, 1)
                for j, dst in enumerate((QR, KR, VR)):
                    split(HEAD_J, j + 2)
                    if j == 2:
                        split(HEAD_J, 5)
                    ready(j)
                    if j < 2:
                        act.wait_ge(s_rope, c.rope.now() + 1)
                    else:
                        act.wait_ge(s_vtok, c.vtok.now() + 1)
                    act.activation(halves(ar(dst, T)), bank2(j % 2), ACT.Copy).then_inc(free[j % 2], 1)
                    c.of("pair", j % 2).next()
                for u, rq, q0, keys, tiles in units():
                    act.wait_ge(s_mx, c.mx.next())
                    if u:
                        act.wait_ge(s_at, c.at.next())
                    for cc in range(2):
                        mm = act.activation(prob[0:rq, cc, 0:keys], ps[0:rq, 4 + cc, 0:keys], ACT.Exp,
                                            bias=nbias[0:rq, cc:cc + 1], scale=SCALE,
                                            accum_out=psum2[0:rq, cc:cc + 1])
                    mm.then_inc(s_exp, 1)
                    if u == 0:
                        ready(3)
                        act.wait_ge(s_bl, c.bl.next() + 4 * l)
                        act.activation(halves(xs), bank2(1), ACT.Copy).then_inc(free[1], 1)
                        c.of("pair", 1).next()
                    elif u == 2:
                        split(HEAD_J, 6)
                        skip(4)
                        c.of("pair", 0).next()
                split(HEAD_J, 7)
                skip(5)
                act.wait_ge(free[1], c.of("pair", 1).next() + 1)
                act.activation(bhi[:, h1, :].rearrange("p a t -> p (a t)"), xs, ACT.Copy).then_inc(s_bh, 1)
                c.at.next()
                c.rope.next(2)
                c.vtok.next()
            act.wait_ge(s_ok, 20 * (l + 1) + 1)
            for b in range(NTT):
                n = P if b < 4 else TS
                for h in range(HEADS):
                    mm = act.activation(ar(VR, P, n), oq[0:n, b, h, :], ACT.Square,
                                        accum_out=osum[0:n, 4 * b + h:4 * b + h + 1])
                    mm.then_inc(s_act, 1)
                    act.wait_ge(s_act, c.act.next())
            act.drain().then_inc(s_osq, 1)
            act.wait_ge(s_ms, c.ms.next())
            act.activation(orms, orms, ACT.Sqrt).then_inc(s_rms, 1)

            for g in range(4):
                split(POOL_J, g + 2)
                ready(g)
                act.wait_ge(s_pad, c.pad.next())
                at = UX + 576 * (g % 2)
                p = g % 2
                act.activation(ar(at + HIST, HALF), ps[:, 2 * p, 0:HALF], ACT.Copy)
                act.activation(ar(at + HIST + HALF, TP - HALF), ps[:, 2 * p + 1, 0:TP - HALF], ACT.Copy)
                act.activation(ar(at + 2 * HIST + TP, TS), ps[:, 2 * p + 1, TP - HALF:HALF],
                               ACT.Copy).then_inc(free[p], 1)
                c.of("pair", p).next()
                act.wait_ge(s_by, c.by.next())
                act.activation(bhi[:, 4 + g, 0:TP], ar(PM + HIST, TP), ACT.Copy)
                act.activation(bhi[:, 4 + g, TP:T], ar(PM + 2 * HIST + TP, TS), ACT.Copy).then_inc(s_bh, 1)
                if g % 2 == 0:
                    continue
                for h in (g - 1, g):
                    act.wait_ge(s_ot, c.ot.next())
                    b = 4 + 2 * (h % 2)
                    act.activation(bhi[:, 8 + h, 0:TP], ps[:, b, 0:TP], ACT.Copy, scale=par[:, R_SUB + l:R_SUB + l + 1])
                    act.activation(bhi[:, 8 + h, TP:T], ps[:, b + 1, 0:TS], ACT.Copy,
                                   scale=par[:, R_SUB + l:R_SUB + l + 1]).then_inc(s_oh, 1)
            with c.trips(4, **turns(12), **seen(12), pair0=6, pair1=6):
                for d2 in range(2):
                    for j, dst, p in ((0, SA, 0), (1, SB_, 1), (2, None, 0), (3, None, 1), (4, SC_, 0), (5, None, 1)):
                        split(GATE_J, 6 * d2 + j + 2)
                        c.of("pair", p).next()
                        if dst is None:
                            skip(6 * d2 + j)
                            continue
                        ready(6 * d2 + j)
                        act.activation(halves(ar(dst, T)), bank2(p), ACT.Sigmoid).then_inc(free[p], 1)
            for k in range(KD):
                act.wait_ge(s_mg, l * KD + k + 1)
                act.activation(bhi[:, k, :], mrg[:, k, :], ACT.Copy).then_inc(s_mh, 1)
            with c.trips(4, **turns(2), **seen(2), pair0=1, pair1=1):
                for j in range(2):
                    split(OUT_J, j + 2)
                    skip(j)
                    c.of("pair", j).next()
            norm_act(True)
            if l == 0:
                with c.trips(2, **both(turns(2, NF), turns(4, 4), seen(2, NF), seen(4, 4)), pair0=NF + 4,
                             pair1=NF + 4):
                    with c.trips(NF, **turns(2), **seen(2), pair0=1, pair1=1) as f:
                        split(UP_J, 2)
                        ready(0)
                        act.activation(halves(ar(FS, T)), bank2(0), ACT.Silu).then_inc(free[0], 1)
                        split(UP_J, 3)
                        skip(1)
                        c.of("pair", 0).next()
                        act.wait_ge(free[1], c.of("pair", 1).next() + 1)
                        act.activation(bhi[:, bass.ds(f, 1), :].rearrange("p a t -> p (a t)"), ar(FA, T),
                                       ACT.Copy).then_inc(s_fh, 1)
                    with c.trips(4, **turns(4), **seen(4), pair0=1, pair1=1):
                        for j in range(4):
                            split(DOWN_J, j + 2)
                            skip(j)
                            if j >= 2:
                                c.of("pair", j - 2).next()

        act.wait_ge(s_wr, 32)
        act.activation(selr[:, 0:64], WR.rearrange("p k e -> p (k e)"), ACT.Copy).then_inc(s_rw, 1)
        n_t = 0
        for j in range(NTT):
            n = P if j < 4 else TS
            for i in range(2):
                for g in range(2):
                    t = 6 * j + 2 * i + g
                    act.wait_ge(s_ht, t + 1)
                    act.activation(htok[i][0:n, j, g * 512:(g + 1) * 512], ps[0:n, 2 + t % 4, :],
                                   ACT.Copy).then_inc(s_hk, 1)
        act.wait_ge(s_re, 1)
        act.activation(R1[2], R1[2], ACT.Exp).then_inc(s_rx, 1)
        act.wait_ge(s_go, 1)
        rounds = act.value_load(rounds_i[0:1, 0:1], min_val=1, max_val=MAXR)
        per = both(turns(len(EXPERT_J)), seen(len(EXPERT_J)), dict(ga=8, st=1, yt=2, pair0=10, pair1=10, pair2=5, pair3=5))
        with c.trips(rounds, **{k: NE * v for k, v in per.items()}):
            with c.trips(NE, **per):
                for d in range(KD):
                    act.wait_ge(s_ga, c.ga.next())
                    act.activation(hg[0][:, d, :], ps[:, 4 + d % 4, 0:CAP], ACT.Copy).then_inc(s_gh, 1)
                act.wait_ge(s_st, c.st.next())
                for a, cn in enumerate(CAPT):
                    act.activation(selT[0:cn, a, 0:TP], ps[0:cn, 4 + 2 * a, :], ACT.Copy)
                    last = act.activation(selT[0:cn, a, TP:T], ps[0:cn, 5 + 2 * a, 0:TS], ACT.Copy)
                last.then_inc(s_stk, 1)
                for f in range(NF):
                    split(EXPERT_J, 2 * f + 2)
                    ready(2 * f)
                    act.activation(ar(ES + CAP * (f % 2), CAP), ps[:, 2 * (f % 2), 0:CAP],
                                   ACT.Silu).then_inc(free[2 * (f % 2)], 1)
                    split(EXPERT_J, 2 * f + 3)
                    skip(2 * f + 1)
                    c.of("pair", 2 * (f % 2)).next()
                    act.wait_ge(free[2 * (f % 2) + 1], c.of("pair", 2 * (f % 2) + 1).next() + 1)
                    act.activation(ea[0][:, f, :], ar(EA + CAP * (f % 2), CAP), ACT.Copy).then_inc(s_fh, 1)
                for m2 in range(4):
                    for q in range(4):
                        j = 2 * NF + 4 * m2 + q
                        split(EXPERT_J, j + 2)
                        if q < 2:
                            skip(j)
                        else:
                            ready(j)
                            act.activation(yT[:, 2 * m2 + q - 2, :], ps[:, q - 2, 0:CAP], ACT.Copy)\
                               .then_inc(free[q - 2], 1)
                            c.of("pair", q - 2).next()
                act.drain().then_inc(s_yd, 8)
                for a, cn in enumerate(CAPT):
                    act.wait_ge(s_yt, c.yt.next())
                    act.activation(ey[0][0:cn, a, :].rearrange("p (g n) -> p g n", g=2),
                                   ps[0:cn, 4 + 2 * a:6 + 2 * a, :], ACT.Copy).then_inc(s_yh, 1)
        act.wait_ge(s_mix, 1)
        for j in range(NTT):
            n = P if j < 4 else TS
            act.activation(ar(EA, D, n), xtok[0:n, j, :], ACT.Square, accum_out=fsum[0:n, j:j + 1]).then_inc(s_act, 1)
            act.wait_ge(s_act, c.act.next())
        act.drain().then_inc(s_fsq, 1)
        act.wait_ge(s_ms, c.ms.next())
        act.activation(frms, frms, ACT.Sqrt).then_inc(s_frm, 1)

    @block.vector
    def _(dve):
        c = Tallies(dve)

        def step(ins):
            ins.then_inc(s_dve, 1)
            dve.wait_ge(s_dve, c.step.next())

        def split(js, p):
            kt = js[p] if p < len(js) else 8
            s = (p if p < len(js) else p - len(js)) % NSLOT
            dve.wait_ge(hi_ready[s], c.of("slot", s).next())
            dve.tensor_tensor(wlo[:, s, 0:kt * P], raw[:, s, 0:kt * P], whi[:, s, 0:kt * P].bitcast(F32),
                              ALU.subtract).then_inc(lo_ready[s], 1)

        def ready(j):
            dve.wait_ge(used[j % NSLOT], c.of("seen", j % NSLOT).next() + 1)

        def skip(j):
            c.of("seen", j % NSLOT).next()

        def seen(n, times=1):
            return {k.replace("slot", "seen"): v for k, v in turns(n, times).items()}

        def norm_dve(gain, cache=None):
            dve.wait_ge(s_sum, c.sum.next(KD))
            dve.tensor_scalar(halves(ar(MS, T)), ps[:, 4:6, 0:HALF], 1.0 / D, EPS, ALU.mult, ALU.add).then_inc(s_ms, 1)
            if cache is not None:
                dve.wait_ge(s_turned, KD + 3 + cache)
                dve.tensor_copy(kpT, ps[:, 6, :].rearrange("p (h t) -> p h t", h=HEADS)).then_inc(s_kept, 1)
            dve.wait_ge(s_rms, c.rms.next())
            step(dve.reciprocal(ar(MS, T), ar(MS, T)))

            def full(k):
                dve.scalar_tensor_tensor(out=ar(HF + T * (k % 2), T), in0=xT[:, k, :],
                                         scalar=par[:, gain + k:gain + k + 1], in1=ar(MS, T),
                                         op0=ALU.mult, op1=ALU.mult).then_inc(s_hf, 1)

            def low(k):
                dve.wait_ge(s_hh, c.hh.next())
                dve.wait_ge(s_hf, c.hf.next())
                dve.tensor_tensor(hlo[:, k, :], ar(HF + T * (k % 2), T), hhi[:, k, :].bitcast(F32),
                                  ALU.subtract).then_inc(s_hl, 1)
                dve.wait_ge(s_hl, c.hl.next())

            full(0)
            for k in range(KD):
                if k + 1 < KD:
                    full(k + 1)
                low(k)

        for s in range(NSLOT):
            dve.sem_inc(lo_ready[s], 1)
        dve.sem_inc(s_rope, 1)
        dve.sem_inc(s_vtok, 1)
        dve.sem_inc(s_ok, 1)
        dve.sem_inc(s_acc, 4)
        dve.sem_inc(s_bl, 1)
        dve.memset(ones[:], 1.0).then_inc(s_ones, 1)
        dve.wait_ge(s_const, 16)
        step(dve.memset(small[:], 1.0))
        dve.wait_ge(s_lam, 64)
        for i in range(2):
            step(dve.tensor_tensor(ar(LAMB + 2 * P * i, P), ar(LAMB + 2 * P * i, P), ar(LAMB + 2 * P * i + P, P), ALU.mult))
            ins = dve.tensor_reduce(lam4[:, 2 * i:2 * i + 2], ar(LAMB + 2 * P * i, P).rearrange("p (l d) -> p l d", l=2),
                                    AX, ALU.add)
            if i == 0:
                step(ins)
        ins.then_inc(s_lamp, 1)
        for k in range(KD):
            dve.wait_ge(s_turned, k + 1)
            b = 2 * (k % 4)
            dve.tensor_copy(xT[:, k, 0:TP], ps[:, b, 0:TP])
            dve.tensor_copy(xT[:, k, TP:T], ps[:, b + 1, 0:TS]).then_inc(s_kept, 1)
        dve.wait_ge(s_turned, KD + 1)
        dve.tensor_copy(par[:], ps[:, 0, 0:R_N]).then_inc(s_kept, 1)
        dve.wait_ge(s_turned, KD + 2)
        dve.tensor_copy(stT[:], ps[:, 1, :].rearrange("p (t n) -> p t n", t=NC4)[:, :, 0:34]).then_inc(s_kept, 1)
        dve.wait_ge(s_lame, 1)
        step(dve.tensor_tensor(neglam, lam4[:, 2:4], lam4[:, 0:2], ALU.subtract))
        for l in range(DEPTH):
            step(dve.tensor_scalar(neglam[:, l:l + 1], neglam[:, l:l + 1], lam_init(l), None, ALU.subtract))
        for s in range(AHEAD):
            split([8, 8], s)
        dve.wait_ge(s_kept, KD + 2)

        for l in range(DEPTH):
            norm_dve(R_MIX + 8 * l, l)

            with c.trips(HEADS, **turns(6), **seen(6), pair0=3, pair1=3, rot=2, vt=1, kt=1, kv=64, sc=5, exp=5, at=5,
                         pv=5, step=29, rope=2, bh=1, bl=1) as h:
                h1 = bass.ds(h, 1)
                for j in range(4):
                    split(HEAD_J, j + 2)
                    skip(j)
                    c.of("pair", j % 2).next()
                for src, dst, b in ((QR, QT, 4), (KR, KT, 6)):
                    dve.wait_ge(s_rot, c.rot.next())
                    dve.tensor_tensor(ar(dst, T), ar(src, T), kc[:, K_COS:K_COS + T], ALU.mult)
                    step(dve.tensor_tensor(halves(ar(TMP, T)), ps[:, b:b + 2, 0:HALF],
                                           halves(kc[:, K_SIN:K_SIN + T]), ALU.mult))
                    dve.tensor_tensor(ar(dst, T), ar(dst, T), ar(TMP, T), ALU.add).then_inc(s_rope, 1)
                    dve.wait_ge(s_rope, c.rope.next() + 1)
                dve.tensor_copy(ar(TMP, PAST), kpT[:, bass.ds(h, 1), :].rearrange("p h t -> p (h t)"))
                dve.wait_ge(s_vt, c.vt.next())
                dve.tensor_copy(vtok[:, 0:4, :], ps[:, 4, :].rearrange("p (j e) -> p j e", j=4))
                dve.tensor_copy(vtok[0:TS, 4, :], ps[0:TS, 5, 0:P]).then_inc(s_vtok, 1)
                dve.wait_ge(s_kt, c.kt.next())
                dve.tensor_copy(ktok[:, 0:4, :], ps[:, 6, :].rearrange("p (j e) -> p j e", j=4))
                dve.tensor_copy(ktok[0:TS, 4, :], ps[0:TS, 7, 0:P]).then_inc(s_ktok, 1)

                def maxima(u, rq, q0, keys, tiles):
                    dve.wait_ge(s_sc, c.sc.next())
                    if u < 4:
                        step(dve.memset(ps[0:64, 4:6, keys - 64:keys], NEG))
                    step(dve.tensor_reduce(smax[0:rq, :], ps[0:rq, 4:6, 0:keys], AX, ALU.max))
                    dve.tensor_scalar(nbias[0:rq, :], smax[0:rq, :], -SCALE, None, ALU.mult).then_inc(s_mx, 1)

                us = list(units())
                maxima(*us[0])
                for u, rq, q0, keys, tiles in us:
                    dve.wait_ge(s_exp, c.exp.next())
                    step(dve.reciprocal(prcp[0:rq, :], psum2[0:rq, :]))
                    step(dve.tensor_tensor(prcp[0:rq, 1:2], prcp[0:rq, 1:2], neglam[0:rq, l:l + 1], ALU.mult))
                    step(dve.tensor_scalar(prob[0:rq, 0, 0:keys], prob[0:rq, 0, 0:keys], prcp[0:rq, 0:1], None, ALU.mult))
                    dve.scalar_tensor_tensor(out=prob[0:rq, 0, 0:keys], in0=prob[0:rq, 1, 0:keys],
                                             scalar=prcp[0:rq, 1:2], in1=prob[0:rq, 0, 0:keys],
                                             op0=ALU.mult, op1=ALU.add).then_inc(s_a, 1)
                    if u < 4:
                        maxima(*us[u + 1])
                    dve.wait_ge(s_at, c.at.next())
                    if u < 4:
                        dve.tensor_copy(ar(AT, keys), ps[:, 6, 0:keys]).then_inc(s_ak, 1)
                    else:
                        dve.tensor_copy(ar(AT, TS), ps[:, 6, 0:TS])
                        dve.tensor_copy(ar(AT + P, TS, TS), ps[0:TS, 6, P:P + TS]).then_inc(s_ak, 1)
                    dve.wait_ge(s_pv, c.pv.next())
                    dve.tensor_copy(oq[0:rq, u, bass.ds(h, 1), :].rearrange("p h e -> p (h e)"),
                                    ps[0:rq, 7, 0:P]).then_inc(s_ok, 1)
                    if u == 1:
                        ready(4)
                        dve.wait_ge(free[1], c.of("pair", 1).now() + 1)
                        dve.memset(ext[:, 0:2], 0.0)
                        dve.tensor_copy(ext[:, TP + 2:TP + 4],
                                        stT[:, h1, 17 * l:17 * l + 2].rearrange("p a n -> p (a n)"))
                        dve.tensor_tensor(ext[:, 2:2 + HALF], ps[:, 0, 0:HALF], xs[:, 0:HALF], ALU.mult)
                        dve.tensor_tensor(ext[:, 2 + HALF:2 + TP], ps[:, 1, 0:TP - HALF], xs[:, HALF:TP], ALU.mult)
                        dve.tensor_tensor(ext[:, TP + 4:], ps[:, 1, TP - HALF:HALF], xs[:, TP:T], ALU.mult)\
                           .then_inc(free[0], 1)
                        c.of("pair", 0).next()
                    elif u == 2:
                        dve.wait_ge(free[0], c.of("pair", 0).now() + 1)
                        dve.tensor_copy(tails[:, h1, 0:2].rearrange("p a n -> p (a n)"), ext[:, TP:TP + 2])
                        dve.tensor_copy(tails[:, h1, 2:4].rearrange("p a n -> p (a n)"), ext[:, T + 2:T + 4])

                        def wj(j):
                            return par[:, bass.ds(h + (R_CW + 12 * l + 4 * j), 1)]
                        step(dve.tensor_scalar(cv, ext[:, 0:T + 2], wj(0), None, ALU.mult))
                        for j in (1, 2):
                            step(dve.scalar_tensor_tensor(out=cv, in0=ext[:, j:T + 2 + j], scalar=wj(j),
                                                          in1=cv, op0=ALU.mult, op1=ALU.add))
                        split(HEAD_J, 6)
                ready(5)
                dve.tensor_tensor(xs[:, 0:HALF], ps[:, 2, 0:HALF], cv[:, 0:HALF], ALU.mult)
                dve.tensor_tensor(xs[:, HALF:TP], ps[:, 3, 0:TP - HALF], cv[:, HALF:TP], ALU.mult)
                dve.tensor_tensor(xs[:, TP:T], ps[:, 3, TP - HALF:HALF], cv[:, TP + 2:T + 2], ALU.mult)\
                   .then_inc(free[1], 1)
                c.of("pair", 1).next()
                split(HEAD_J, 7)
                dve.wait_ge(s_bh, c.bh.next())
                dve.tensor_tensor(blo[:, h1, :].rearrange("p a t -> p (a t)"), xs,
                                  bhi[:, h1, :].rearrange("p a t -> p (a t)").bitcast(F32),
                                  ALU.subtract).then_inc(s_bl, 1)
                dve.wait_ge(s_bl, c.bl.next() + 1)
                dve.wait_ge(s_kv, c.kv.next(64))

            dve.wait_ge(s_osq, l + 1)
            dve.tensor_scalar(orms, osum, 1.0 / P, SUB_EPS, ALU.mult, ALU.add).then_inc(s_ms, 1)
            dve.wait_ge(s_rms, c.rms.next())
            step(dve.reciprocal(orms, orms))
            step(dve.tensor_scalar(orms, orms, 1.0 - lam_init(l), None, ALU.mult))
            for b in range(NTT):
                n = P if b < 4 else TS
                last = dve.tensor_tensor(oq[0:n, b, :, :], oq[0:n, b, :, :],
                                         orms[0:n, 4 * b:4 * b + 4].rearrange("p (h a) -> p h a", a=1)
                                         .broadcast_to([n, HEADS, P]), ALU.mult)
            last.then_inc(s_on, 1)

            for g in range(4):
                at = UX + 576 * (g % 2)
                dve.memset(ar(at, HIST), 0.0)
                dve.tensor_copy(ar(at + HIST + TP, HIST), stT[:, g, 17 * l + 2:17 * l + 17]).then_inc(s_pad, 1)
                split(POOL_J, g + 2)
                skip(g)
                p = g % 2
                c.of("pair", p).next()
                dve.wait_ge(free[p], c.of("pair", p).now() + 1)
                dve.tensor_copy(tails[:, g, 4:19], ar(at + TP, HIST))
                dve.tensor_copy(tails[:, g, 19:34], ar(at + TP + HIST + TS, HIST))
                n, lag, src = 574, 1, at
                for i in range(g + 1):
                    dst = (PA, PB)[i % 2]
                    first = 2 * lag - 1
                    step(dve.tensor_tensor(ar(dst + first, n - first), ar(src + first, n - first),
                                           ar(src + first - lag, n - first), ALU.add))
                    src, lag = dst, 2 * lag
                step(dve.scalar_tensor_tensor(out=ar(PM + HIST, n - HIST), in0=ar(src + HIST, n - HIST),
                                              scalar=1.0 / lag, in1=ar(at + HIST, n - HIST),
                                              op0=ALU.mult, op1=ALU.subtract))
                step(dve.tensor_tensor(ar(PM + HIST, HIST), ar(src + HIST, HIST),
                                       kc[:, K_RC + HIST * g:K_RC + HIST * (g + 1)], ALU.mult))
                dve.tensor_tensor(ar(PM + HIST, HIST), ar(PM + HIST, HIST), ar(at + HIST, HIST),
                                  ALU.subtract).then_inc(s_by, 1)
                dve.wait_ge(s_bh, c.bh.next())
                dve.tensor_tensor(blo[:, 4 + g, 0:TP], ar(PM + HIST, TP), bhi[:, 4 + g, 0:TP].bitcast(F32), ALU.subtract)
                dve.tensor_tensor(blo[:, 4 + g, TP:T], ar(PM + 2 * HIST + TP, TS),
                                  bhi[:, 4 + g, TP:T].bitcast(F32), ALU.subtract).then_inc(s_bl, 1)
                dve.wait_ge(s_bl, c.bl.next() + 1)
                if g % 2 == 0:
                    continue
                for h in (g - 1, g):
                    dve.wait_ge(s_oh, c.oh.next())
                    b = 4 + 2 * (h % 2)
                    gain = par[:, R_SUB + l:R_SUB + l + 1]
                    dve.scalar_tensor_tensor(out=blo[:, 8 + h, 0:TP], in0=ps[:, b, 0:TP], scalar=gain,
                                             in1=bhi[:, 8 + h, 0:TP].bitcast(F32), op0=ALU.mult, op1=ALU.subtract)
                    dve.scalar_tensor_tensor(out=blo[:, 8 + h, TP:T], in0=ps[:, b + 1, 0:TS], scalar=gain,
                                             in1=bhi[:, 8 + h, TP:T].bitcast(F32), op0=ALU.mult,
                                             op1=ALU.subtract).then_inc(s_ol, 1)
            with c.trips(4, **turns(12), **seen(12), pair0=6, pair1=6, step=2, mg=2) as g:
                for d2 in range(2):
                    md = mrg[:, bass.ds(g * 2 + d2, 1), :].rearrange("p a t -> p (a t)")
                    for j in range(6):
                        split(GATE_J, 6 * d2 + j + 2)
                        p = j % 2
                        c.of("pair", p).next()
                        if j in (0, 1, 4):
                            skip(6 * d2 + j)
                            continue
                        ready(6 * d2 + j)
                        if j == 2:
                            dve.wait_ge(free[0], c.of("pair", 0).now())
                            dve.tensor_tensor(halves(md), bank2(0), halves(ar(SA, T)), ALU.mult).then_inc(free[0], 1)
                            dve.wait_ge(free[0], c.of("pair", 0).now() + 1)
                        elif j == 3:
                            dve.wait_ge(free[1], c.of("pair", 1).now())
                            ins = dve.scalar_tensor_tensor(
                                out=halves(ar(GT, T)), in0=bank2(1),
                                scalar=par[:, bass.ds(g * 2 + (R_PS + 8 * l + d2), 1)],
                                in1=halves(ar(SB_, T)), op0=ALU.mult, op1=ALU.mult)
                            ins.then_inc(free[1], 1)
                            dve.wait_ge(free[1], c.of("pair", 1).now() + 1)
                            step(dve.tensor_tensor(md, md, ar(GT, T), ALU.add))
                        else:
                            dve.wait_ge(free[0], c.of("pair", 0).now() + 1)
                            dve.tensor_tensor(halves(ar(GT, T)), bank2(1), halves(ar(SC_, T)), ALU.mult)\
                               .then_inc(free[1], 1)
                            dve.wait_ge(free[1], c.of("pair", 1).now() + 1)
                            dve.tensor_tensor(md, md, ar(GT, T), ALU.add).then_inc(s_mg, 1)
                            dve.wait_ge(s_mg, c.mg.next())
            for k in range(KD):
                dve.wait_ge(s_mh, c.mh.next())
                dve.tensor_tensor(blo[:, k, :], mrg[:, k, :], bhi[:, k, :].bitcast(F32), ALU.subtract).then_inc(s_ml, 1)
            dve.wait_ge(s_tt, l + 1)
            dve.tensor_copy(ar(TROW, 512, 34), ps[0:34, 6, :]).then_inc(s_tk, 1)
            with c.trips(4, **turns(2), **seen(2), pair0=1, pair1=1) as m2:
                for j in range(2):
                    split(OUT_J, j + 2)
                    ready(j)
                    xd = halves(xT[:, bass.ds(m2 * 2 + j, 1), :].rearrange("p a t -> p (a t)"))
                    dve.tensor_tensor(xd, bank2(j), xd, ALU.add).then_inc(free[j], 1)
                    c.of("pair", j).next()
            dve.drain().then_inc(s_xr, 1)
            dve.wait_ge(s_ts, 64 * (l + 1))
            norm_dve(R_FFN + 8 * l)
            if l == 0:
                with c.trips(2, **both(turns(2, NF), turns(4, 4), seen(2, NF), seen(4, 4)), pair0=NF + 4,
                             pair1=NF + 4, fh=NF, fl=NF):
                    with c.trips(NF, **turns(2), **seen(2), pair0=1, pair1=1, fh=1, fl=1) as f:
                        split(UP_J, 2)
                        skip(0)
                        split(UP_J, 3)
                        ready(1)
                        dve.wait_ge(free[0], c.of("pair", 0).next() + 1)
                        dve.tensor_tensor(halves(ar(FA, T)), bank2(1), halves(ar(FS, T)), ALU.mult).then_inc(free[1], 1)
                        dve.wait_ge(free[1], c.of("pair", 1).next() + 1)
                        dve.wait_ge(s_fh, c.fh.next())
                        dve.tensor_tensor(blo[:, bass.ds(f, 1), :].rearrange("p a t -> p (a t)"), ar(FA, T),
                                          bhi[:, bass.ds(f, 1), :].rearrange("p a t -> p (a t)").bitcast(F32),
                                          ALU.subtract).then_inc(s_fl, 1)
                        dve.wait_ge(s_fl, c.fl.next())
                    with c.trips(4, **turns(4), **seen(4), pair0=1, pair1=1) as m2:
                        for j in range(4):
                            split(DOWN_J, j + 2)
                            if j < 2:
                                skip(j)
                                continue
                            ready(j)
                            xd = halves(xT[:, bass.ds(m2 * 2 + (j - 2), 1), :].rearrange("p a t -> p (a t)"))
                            dve.tensor_tensor(xd, bank2(j - 2), xd, ALU.add).then_inc(free[j - 2], 1)
                            c.of("pair", j - 2).next()
                dve.drain().then_inc(s_xr, 1)

        dve.wait_ge(s_rw, 1)
        dve.tensor_tensor(selr[:, 64:128], WR.rearrange("p k e -> p (k e)"), selr[:, 0:64].bitcast(F32),
                          ALU.subtract).then_inc(s_rw, 1)
        dve.wait_ge(s_lg, 1)
        for t in (LG, RM, WT, T1, T2):
            dve.memset(t, 0.0)
        step(dve.memset(EQ, 0.0))
        step(dve.tensor_tensor(LG[:, 0:4, :], ps[:, 0, 0:32].rearrange("p (j e) -> p j e", j=4),
                               BR.rearrange("p (j e) -> p j e", j=1).broadcast_to([P, 4, NE]), ALU.add))
        step(dve.tensor_tensor(LG[0:TS, 4, :], ps[0:TS, 0, 32:40], BR[0:TS, :], ALU.add))

        def e3(ap):
            return ap.rearrange("p (j a) -> p j a", a=1).broadcast_to([P, NTT, NE])
        rank = kc[:, K_RANK:K_RANK + NE].rearrange("p (a e) -> p a e", a=1).broadcast_to([P, NTT, NE])

        def first_max(m, top, oh):
            step(dve.tensor_reduce(top, m, AX, ALU.max))
            step(dve.tensor_tensor(EQ, m, e3(top), ALU.is_equal))
            step(dve.tensor_tensor(EQ, EQ, rank, ALU.mult))
            step(dve.tensor_reduce(R1[3], EQ, AX, ALU.max))
            step(dve.tensor_tensor(oh, EQ, e3(R1[3]), ALU.is_equal))
        first_max(LG, R1[0], OH1)
        step(dve.scalar_tensor_tensor(out=T1, in0=OH1, scalar=BIG, in1=LG, op0=ALU.mult, op1=ALU.add))
        first_max(T1, R1[1], OH2)
        dve.tensor_tensor(R1[2], R1[1], R1[0], ALU.subtract).then_inc(s_re, 1)
        step(dve.tensor_tensor(T2, OH1, OH2, ALU.add))
        dve.tensor_copy(RM[:, 0:4, :], T2[:, 0:4, :])
        dve.tensor_copy(RM[0:TS, 4, :], T2[0:TS, 4, :]).then_inc(s_rt, 1)
        for j in range(NTT):
            n = P if j < 4 else TS
            for g in range(2):
                t = 6 * j + 4 + g
                dve.wait_ge(s_ht, t + 1)
                dve.tensor_copy(xtok[0:n, j, g * 512:(g + 1) * 512], ps[0:n, 2 + t % 4, :]).then_inc(s_hkd, 1)
        dve.wait_ge(s_rx, 1)
        step(dve.tensor_scalar(R1[3], R1[2], 1.0, None, ALU.add))
        step(dve.reciprocal(R1[3], R1[3]))
        step(dve.tensor_tensor(R1[4], R1[2], R1[3], ALU.mult))
        step(dve.tensor_tensor(T1, OH1, e3(R1[3]), ALU.mult))
        step(dve.tensor_tensor(T2, OH2, e3(R1[4]), ALU.mult))
        step(dve.tensor_tensor(WT, T1, T2, ALU.add))
        dve.wait_ge(s_pos, 1)
        step(dve.memset(SL, -1.0))
        step(dve.tensor_tensor(SL[:, 0:4, :], ps[:, 6, 0:32].rearrange("p (j e) -> p j e", j=4), RM[:, 0:4, :], ALU.mult))
        step(dve.tensor_tensor(SL[0:TS, 4, :], ps[0:TS, 6, 32:40], RM[0:TS, 4, :], ALU.mult))
        step(dve.tensor_scalar(SL[:, 0:4, :], SL[:, 0:4, :], -1.0, None, ALU.add))
        step(dve.tensor_scalar(SL[0:TS, 4, :], SL[0:TS, 4, :], -1.0, None, ALU.add))
        step(dve.tensor_reduce(rmaxc, ps[:, 7, 0:8], AX, ALU.max))
        step(dve.memset(rtmp, 0.0))
        for r in range(1, MAXR):
            step(dve.tensor_scalar(rtmp[:, r - 1:r], rmaxc, float(r * CAP), None, ALU.is_gt))
        step(dve.tensor_reduce(rnd, rtmp, AX, ALU.add))
        step(dve.tensor_scalar(rnd, rnd, 1.0, None, ALU.add))
        dve.tensor_copy(rounds_i[:, 0:1], rnd).then_inc(s_go, 1)
        dve.wait_ge(s_go, 1)
        dve.wait_ge(s_hkd, 10)
        rounds = dve.value_load(rounds_i[0:1, 0:1], min_val=1, max_val=MAXR)
        per = both(turns(len(EXPERT_J)), seen(len(EXPERT_J)),
                   dict(pair0=10, pair1=10, pair2=5, pair3=5, gh=8, fh=NF, yh=2, sp=10, fl=NF))
        outer = {k: NE * v for k, v in per.items()}
        with c.trips(rounds, **outer, step=1):
            with c.trips(NE, **per) as e:
                e1 = bass.ds(e, 1)
                for j in range(NTT):
                    n = P if j < 4 else TS
                    ins = dve.tensor_scalar(sel[0:n, j, :], kc[0:n, K_IOTA:K_IOTA + CAP],
                                            SL[0:n, j, e1], None, ALU.is_equal)
                ins.then_inc(s_sel, 1)
                for d in range(KD):
                    dve.wait_ge(s_gh, c.gh.next())
                    dve.tensor_tensor(hg[1][:, d, :], ps[:, 4 + d % 4, 0:CAP], hg[0][:, d, :].bitcast(F32),
                                      ALU.subtract).then_inc(s_gl, 1)
                for f in range(NF):
                    split(EXPERT_J, 2 * f + 2)
                    skip(2 * f)
                    split(EXPERT_J, 2 * f + 3)
                    ready(2 * f + 1)
                    p = 2 * (f % 2)
                    dve.wait_ge(free[p], c.of("pair", p).next() + 1)
                    dve.tensor_tensor(ar(EA + CAP * (f % 2), CAP), ps[:, p + 1, 0:CAP],
                                      ar(ES + CAP * (f % 2), CAP), ALU.mult).then_inc(free[p + 1], 1)
                    dve.wait_ge(free[p + 1], c.of("pair", p + 1).next() + 1)
                    dve.wait_ge(s_fh, c.fh.next())
                    dve.tensor_tensor(ea[1][:, f, :], ar(EA + CAP * (f % 2), CAP), ea[0][:, f, :].bitcast(F32),
                                      ALU.subtract).then_inc(s_fl, 1)
                    c.fl.next()
                for m2 in range(4):
                    for q in range(4):
                        j = 2 * NF + 4 * m2 + q
                        split(EXPERT_J, j + 2)
                        skip(j)
                        if q >= 2:
                            c.of("pair", q - 2).next()
                for a, cn in enumerate(CAPT):
                    dve.wait_ge(s_yh, c.yh.next())
                    dve.tensor_tensor(ey[1][0:cn, a, :].rearrange("p (g n) -> p g n", g=2),
                                      ps[0:cn, 4 + 2 * a:6 + 2 * a, :],
                                      ey[0][0:cn, a, :].bitcast(F32).rearrange("p (g n) -> p g n", g=2),
                                      ALU.subtract).then_inc(s_yl, 1)
                for n in range(2 * NTT):
                    j, g = n // 2, n % 2
                    rows_ = P if j < 4 else TS
                    dve.wait_ge(s_sp, c.sp.next())
                    xd = xtok[0:rows_, j, g * 512:(g + 1) * 512]
                    dve.scalar_tensor_tensor(out=xd, in0=ps[0:rows_, 4 + n % 4, :], scalar=WT[0:rows_, j, e1],
                                             in1=xd, op0=ALU.mult, op1=ALU.add).then_inc(s_acc, 1)
            step(dve.tensor_scalar(SL, SL, float(CAP), None, ALU.subtract))
        dve.drain().then_inc(s_mix, 1)
        dve.wait_ge(s_fsq, 1)
        dve.tensor_scalar(frms, fsum, 1.0 / D, EPS, ALU.mult, ALU.add).then_inc(s_ms, 1)
        dve.wait_ge(s_frm, 1)
        dve.reciprocal(frms, frms).then_inc(s_frm, 1)
        dve.wait_ge(s_frm, 2)
        dve.wait_ge(s_gf, 16)
        for j in range(NTT):
            n = P if j < 4 else TS
            dve.scalar_tensor_tensor(out=xtok[0:n, j, :], in0=xtok[0:n, j, :], scalar=frms[0:n, j:j + 1],
                                     in1=ar(GF, D, n), op0=ALU.mult, op1=ALU.mult).then_inc(s_fin, 1)

    ctx.close()


_INS = ['x_prompt', 'x_sample', 'cache_k', 'cache_v', 'state_conv', 'state_pool', 'norm_mix', 'w_in', 'conv_w',
        'w_conv_out', 'w_pool', 'pool_scale', 'lambda_q1', 'lambda_k1', 'lambda_q2', 'lambda_k2', 'subln_g',
        'w_attn_out', 'w_o', 'norm_ffn', 'w_gate_d', 'w_up_d', 'w_down_d', 'w_router', 'b_router', 'w_gate_e',
        'w_up_e', 'w_down_e', 'norm_final']
_OUTS = [(1, 512, 1024), (1, 32, 1024), (2, 1, 512, 4, 128), (2, 1, 512, 4, 128), (2, 1, 2, 512), (2, 1, 15, 512),
         (2, 1, 32, 4, 128), (2, 1, 32, 4, 128), (2, 1, 2, 512), (2, 1, 15, 512)]


def constants(np):
    k = np.zeros((P, K_N), np.float32)
    pos = np.concatenate([np.arange(TP), PAST + np.arange(TS)]).astype(np.float32)
    half = 32
    freq = np.float32(10000.0) ** (-np.arange(half, dtype=np.float32) / np.float32(half))
    ang = (freq[:, None].astype(np.float32) * pos[None, :]).astype(np.float32)
    k[:, K_COS:K_COS + T] = np.tile(np.cos(ang), (4, 1))
    k[:, K_SIN:K_SIN + T] = np.tile(np.sin(ang), (4, 1))
    k[:, K_ID:K_ID + P] = np.eye(P)
    for p in range(P):
        if p % 64 < 32:
            k[p + 32, K_ROT + p] = -1.0
        else:
            k[p - 32, K_ROT + p] = 1.0
    k[:, K_TRI:K_TRI + P] = np.triu(np.ones((P, P)))
    k[:, K_IOTA:K_IOTA + CAP] = np.arange(CAP)[None, :]
    for g in range(4):
        k[:, K_RC + HIST * g:K_RC + HIST * (g + 1)] = 1.0 / np.minimum(np.arange(HIST) + 1, 2 ** (g + 1))
    k[:, K_RANK:K_RANK + NE] = NE - np.arange(NE)
    return k


def kernel(**inputs):
    import numpy as _np
    import concourse.bacc as _bacc
    from concourse import mybir as _mybir
    from concourse.bass_utils import run_bass_kernel_spmd as _run

    nc = _bacc.Bacc("TRN2", target_bir_lowering=False, num_devices=1)
    arrays, args = {}, []
    for name in _INS:
        a = _np.ascontiguousarray(inputs[name])
        arrays[f"in_{name}_dram"] = a
        args.append(nc.dram_tensor(f"in_{name}_dram", a.shape, _mybir.dt.from_np(a.dtype), kind="ExternalInput").ap())
    a = constants(_np)
    arrays["in_consts_dram"] = a
    args.append(nc.dram_tensor("in_consts_dram", a.shape, _mybir.dt.float32, kind="ExternalInput").ap())
    for i, shape in enumerate(_OUTS):
        args.append(nc.dram_tensor(f"out_{i}_dram", shape, _mybir.dt.float32, kind="ExternalOutput").ap())
    program(nc, *args)
    r = _run(nc, [arrays], core_ids=[0])
    return tuple(r.results[0][f"out_{i}_dram"] for i in range(len(_OUTS)))
```

```python
from contextlib import ExitStack, contextmanager
import math

import concourse.bass as bass
from concourse import mybir

P = 128
F32 = mybir.dt.float32
F32R = mybir.dt.float32r
I32 = mybir.dt.int32
ALU = mybir.AluOpType
ACT = mybir.ActivationFunctionType
AX = mybir.AxisListType.X

D = 1024
KD = D // P
TP, TS = 512, 32
T = TP + TS
HALF = T // 2
QUARTER = T // 4
NTT = 5
DEPTH = 2
PAST = 128
HEADS = 4
CW = 512
NC4 = CW // P
HIST = 15
FE = 1408
NF = FE // P
NE = 8
CAP = 208
CAPT = (128, CAP - 128)
MAXR = -(-T // CAP)
SPREAD = (4, 6, 5, 7)
GATHER = (5, 7, 4, 6)
EPS = 1e-6
SUB_EPS = 1e-5
SCALE = 0.125
NEG = -1.0e30
BIG = -3.0e38

C_X, C_B, C_C, C_U, C_Q, C_K, C_V, C_G = (0, 512, 1024, 1536, 2048, 2560, 3072, 3584)

K_COS, K_SIN, K_ID, K_ROT, K_TRI, K_IOTA = 0, 544, 1088, 1216, 1344, 1472
K_RC, K_RANK = K_IOTA + CAP, K_IOTA + CAP + 4 * HIST
K_N = K_RANK + NE

R_MIX, R_FFN, R_PS, R_CW, R_SUB = 0, 16, 32, 48, 72
R_N = 74

NSLOT = 4
AHEAD = 2
AHEAD_E = NSLOT


MIX_PAIRS = 3 * HEADS + 2 + 6 * 4 + 4
FFN_PAIRS = 2 * (NF + 4)


def lam_init(l):
    return 0.8 - 0.6 * math.exp(-0.3 * l)


class Tally:

    def __init__(self, base=0):
        self.base, self.off = base, 0

    def now(self):
        return self.base + self.off

    def next(self, k=1):
        self.off += k
        return self.now()


class Tallies:

    def __init__(self, eng):
        self.eng, self.all = eng, {}

    def __getattr__(self, name):
        return self.all.setdefault(name, Tally())

    def of(self, name, i):
        return self.all.setdefault(f"{name}{i}", Tally())

    @contextmanager
    def trips(self, n, **per):
        for k in per:
            self.all.setdefault(k, Tally())
        saved = {k: (t.base, t.off) for k, t in self.all.items()}
        with self.eng.Fori(0, n) as i:
            for k, t in self.all.items():
                if per.get(k, 0):
                    t.base = t.base + t.off + i * per[k]
                    t.off = 0
            yield i
            got = {k: t.off - (0 if per.get(k, 0) else saved.get(k, (0, 0))[1]) for k, t in self.all.items()}
            bad = {k: (v, per.get(k, 0)) for k, v in got.items() if v != per.get(k, 0)}
            assert not bad, bad
        for k, t in self.all.items():
            b, o = saved.get(k, (0, 0))
            t.base, t.off = b, o + (n * per.get(k, 0) if isinstance(n, int) else 0)


def turns(jobs, times=1):
    return {f"slot{s}": times * len(range(s, jobs, NSLOT)) for s in range(NSLOT)}


def both(*parts):
    out = {}
    for p in parts:
        for k, v in p.items():
            out[k] = out.get(k, 0) + v
    return out


HEAD_J = [8] * 6
POOL_J = [8, 8, 8, 8]
GATE_J = [8, 8, 4, 1, 8, 4] * 2
OUT_J = [8, 8]
UP_J = [8, 8]
DOWN_J = [8, 8, NF - 8, NF - 8]
EXPERT_J = [8] * (2 * NF) + DOWN_J * 4


def refill(j):
    n, odd = len(EXPERT_J), len(EXPERT_J) % NSLOT
    return j + NSLOT if j < n - NSLOT else n + (j - (n - NSLOT) + odd) % NSLOT


def program(nc, x_prompt, x_sample, cache_k, cache_v, state_conv, state_pool, norm_mix, w_in, conv_w, w_conv_out,
            w_pool, pool_scale, lambda_q1, lambda_k1, lambda_q2, lambda_k2, subln_g, w_attn_out, w_o, norm_ffn,
            w_gate_d, w_up_d, w_down_d, w_router, b_router, w_gate_e, w_up_e, w_down_e, norm_final, consts,
            y_prompt, y_sample, k_prompt, v_prompt, conv_prompt, pool_prompt, k_sample, v_sample, conv_sample,
            pool_sample):
    ctx = ExitStack()

    def sb(name, shape, dt=F32):
        return ctx.enter_context(nc.sbuf_tensor(name, shape, dt))

    def sem(name):
        return ctx.enter_context(nc.semaphore(name))

    raw = sb("raw", [P, NSLOT, 1024])
    whi = sb("whi", [P, NSLOT, 1024], F32R)
    wlo = sb("wlo", [P, NSLOT, 1024], F32R)
    hpair = sb("hpair", [P, 2, KD, T], F32R)
    hhi, hlo = hpair[:, 0], hpair[:, 1]
    bhi = sb("bhi", [P, 12, T], F32R)
    blo = sb("blo", [P, 12, T], F32R)
    with nc.sbuf_tensor("conv_work", [P, 3 * T + 6], F32) as conv_work:
        pass
    selr = sb("selr", [P, NTT * CAP + 2 * T], F32R)
    xT = sb("xT", [P, KD, T])
    arena = sb("arena", [P, 9664])
    kc = sb("kc", [P, K_N])
    par = sb("par", [P, R_N])
    ones = sb("ones", [P, P])
    band = sb("band", [P, 2 * P - 32])
    stT = sb("stT", [P, NC4, 34])
    tails = sb("tails", [P, NC4, 34])
    small = sb("small", [P, 64])
    rounds_i = sb("rounds_i", [P, 2], I32)
    ps = ctx.enter_context(nc.psum_tensor("ps", [P, 8, 512], F32))

    def ar(at, n, rows=P):
        return arena[0:rows, at:at + n]

    ident = kc[:, K_ID:K_ID + P]
    neglam = small[:, 0:2]
    smax = small[:, 2:4]
    nbias = small[:, 4:6]
    psum2 = small[:, 6:8]
    prcp = small[:, 8:10]
    osum = small[:, 10:30]
    orms = small[:, 30:50]
    lam4 = small[:, 50:54]
    fsum = small[:, 54:59]
    frms = small[:, 59:64]

    landed = [sem(f"landed{s}") for s in range(NSLOT)]
    hi_ready = [sem(f"hi_ready{s}") for s in range(NSLOT)]
    lo_ready = [sem(f"lo_ready{s}") for s in range(NSLOT)]
    used = [sem(f"used{s}") for s in range(NSLOT)]
    free = [sem(f"result_free{p}") for p in range(4)]
    s_ident, s_const, s_rows, s_lam, s_state = (sem(n) for n in ("identity_in", "const_in", "rows_in", "lambda_in",
                                                                 "state_in"))
    s_x = [sem(f"x_in{j}") for j in range(NTT)]
    s_cache = sem("cache_in")
    s_ones = sem("ones_set")
    s_pace = sem("pace")
    s_turned = sem("input_turned")
    s_kept = sem("input_kept")
    s_lamp = sem("lambda_products")
    s_lame = sem("lambda_exp")
    s_dve = sem("dve_step")
    s_act = sem("act_step")
    s_sq = sem("squares")
    s_sqp = sem("squares_paired")
    s_pool = sem("pool_step")
    s_sq7 = sem("squares_of_seven")
    s_sum = sem("squares_summed")
    s_ms = sem("mean_square")
    s_rms = sem("root_mean_square")
    s_rcp = sem("reciprocal_root")
    s_rin = sem("reciprocal_spread")
    s_hf = sem("h_full")
    s_hh = sem("h_hi")
    s_hl = sem("h_lo")
    s_hlo = sem("h_lo_odd")
    s_rot = sem("rotated")
    s_rope = sem("rope_done")
    s_vt = sem("v_turned")
    s_vtok = sem("v_tokens")
    s_kt = sem("k_turned")
    s_ktok = sem("k_tokens")
    s_kv = sem("kv_stored")
    s_sc = sem("scores")
    s_mx = sem("score_max")
    s_exp = sem("probabilities")
    s_a = sem("difference")
    s_at = sem("difference_turned")
    s_ak = sem("difference_kept")
    s_pv = sem("attended")
    s_ok = sem("attended_kept")
    s_osq = sem("attended_squares")
    s_on = sem("attended_normed")
    s_ot = sem("attended_turned")
    s_oh = sem("attended_hi")
    s_ol = sem("attended_lo")
    s_by = sem("branch_full")
    s_bh = sem("branch_hi")
    s_bl = sem("branch_lo")
    s_pad = sem("pool_pads")
    s_tt = sem("tails_turned")
    s_tk = sem("tails_kept")
    s_ts = sem("tails_stored")
    s_mg = sem("merged")
    s_mh = sem("merged_hi")
    s_ml = sem("merged_lo")
    s_xr = sem("residual_ready")
    s_fh = sem("hidden_hi")
    s_fl = sem("hidden_lo")
    s_wr = sem("router_in")
    s_rw = sem("router_split")
    s_lge = sem("logits_by_expert")
    s_lgk = sem("logits_kept")
    s_lg = sem("logits")
    s_rt = sem("routes")
    s_re = sem("route_exp_in")
    s_rx = sem("route_exp")
    s_pos = sem("positions")
    s_go = sem("rounds_known")
    s_ht = sem("rows_turned")
    s_hk = sem("rows_kept_act")
    s_hkd = sem("rows_kept_dve")
    s_sel = sem("selection")
    s_ga = sem("gathered")
    s_gh = sem("gathered_hi")
    s_gl = sem("gathered_lo")
    s_st = sem("selection_turned")
    s_stk = sem("selection_turned_kept")
    s_si = sem("silu")
    s_em = sem("expert_hidden")
    s_yt = sem("expert_out_turned")
    s_yh = sem("expert_out_hi")
    s_yl = sem("expert_out_lo")
    s_sp = sem("spread")
    s_acc = sem("spread_added")
    s_mix = sem("experts_added")
    s_fsq = sem("final_squares")
    s_frm = sem("final_root")
    s_fin = sem("final_rows")
    s_gf = sem("final_gain_in")
    s_out = sem("outputs_stored")

    block = ctx.enter_context(nc.Block())

    XIN = 0
    ROWS = 5120
    STROWS = ROWS + P
    LAMB = STROWS + 512
    QR, KR, VR, TMP, QT, KT = 0, 544, 1088, 1632, 2176, 2720
    VTOK, KTOK, PROB, AT, OQ, KPT, VP = 3264, 3904, 4544, 5568, 6080, 8640, 9152
    SQ, MS, HF = 0, 5120, 6460
    UX, PA, PB, PM = 2224, 3376, 3952, 0
    TROW = 6528
    M, SA, SB_, SC_, GT = 0, 4352, 4896, 5440, 5984
    FS, FA = 4352, 4896
    XTOK, YT = 0, NTT * D
    ES = YT + KD * CAP
    EA = ES + 2 * CAP
    RT = EA + 2 * CAP
    GF = YT

    xs, ext, cv = (conv_work[:, a:a + n] for a, n in ((0, T), (T, T + 4), (2 * T + 4, T + 2)))
    oq = ar(OQ, NTT * HEADS * P).rearrange("p (b h e) -> p b h e", b=NTT, h=HEADS)
    prob = ar(PROB, 1024).rearrange("p (c n) -> p c n", c=2)
    vtok = ar(VTOK, NTT * P).rearrange("p (j e) -> p j e", j=NTT)
    ktok = ar(KTOK, NTT * P).rearrange("p (j e) -> p j e", j=NTT)
    kpT = ar(KPT, 512).rearrange("p (h t) -> p h t", h=HEADS)
    vpast = ar(VP, 512).rearrange("p (h e) -> p h e", h=HEADS)
    mrg = ar(M, KD * T).rearrange("p (k t) -> p k t", k=KD)
    xtok = ar(XTOK, NTT * D).rearrange("p (j d) -> p j d", j=NTT)
    yT = ar(YT, KD * CAP).rearrange("p (k c) -> p k c", k=KD)

    htok = [t[:, :, :].rearrange("p k t -> p (k t)")[:, 0:NTT * D].rearrange("p (j d) -> p j d", j=NTT)
            for t in (bhi, blo)]
    hflat = hpair[:, :, :, :].rearrange("p i k t -> p i (k t)")
    hg = hflat[:, :, NF * CAP:(NF + KD) * CAP].rearrange("p i (k c) -> p i k c", k=KD)
    ea = hflat[:, :, 0:NF * CAP].rearrange("p i (k c) -> p i k c", k=NF)
    ey = hflat[:, :, 0:2 * D].rearrange("p i (a d) -> p i a d", a=2)
    sel = selr[:, 0:NTT * CAP].rearrange("p (j c) -> p j c", j=NTT)
    selT = selr[:, NTT * CAP:].rearrange("p (a t) -> p a t", a=2)
    LGT = ar(ES, T, NE)
    def rt(i):
        return ar(RT + 40 * i, 40).rearrange("p (j e) -> p j e", j=NTT)
    LG, EQ, OH1, OH2, RM, WT, T1, T2, SL = (rt(i) for i in range(9))
    R1 = ar(RT + 400, 5), ar(RT + 405, 5), ar(RT + 410, 5), ar(RT + 415, 5), ar(RT + 420, 5)
    rmaxc = ar(RT + 433, 1)
    rnd = ar(RT + 434, 1)
    rtmp = ar(RT + 435, 3)
    BR = ar(GT, 8)
    WR = ar(GT + 8, 64).rearrange("p (k e) -> p k e", k=KD)

    def bank2(p):
        return ps[:, 2 * p:2 * p + 2, 0:HALF]

    def halves(ap):
        return ap.rearrange("p (a n) -> p a n", a=2)

    def kview(w):
        return w.rearrange("(k p) n -> p k n", p=P)

    def units():
        for b in range(4):
            yield b, P, b * P, (b + 1) * P, [P] * (b + 1)
        yield 4, TS, TP, PAST + TS, [PAST, TS]

    @block.sync
    def _(sp):
        c = Tallies(sp)
        pos = [0]

        def load(src, kt, alone=False):
            s = pos[0] % NSLOT
            pos[0] += 1
            n = c.of("slot", s).next()
            sp.wait_ge(lo_ready[s], n)
            if alone:
                sp.sem_inc(s_pace, 1)
            sp.dma_start(raw[:, s, 0:kt * P].rearrange("p (k n) -> p k n", k=kt), src).then_inc(landed[s], 16)

        sp.dma_start(ident, consts[:, K_ID:K_ID + P]).then_inc(s_ident, 16)
        for j in range(4):
            sp.dma_start(ar(XIN + j * D, D), x_prompt[0, j * P:(j + 1) * P]).then_inc(s_x[j], 16)
        sp.dma_start(ar(XIN + 4096, D, TS), x_sample[0]).then_inc(s_x[4], 16)
        sp.dma_start(kc[:, K_ID + P:K_N], consts[:, K_ID + P:K_N]).then_inc(s_const, 16)
        sp.dma_start(kc[:, 0:K_ID], consts[:, 0:K_ID]).then_inc(s_const, 16)

        for l in range(DEPTH):
            w = w_in[l]
            with c.trips(HEADS, **turns(6)) as h:
                pos[0] = 0
                for col in (C_Q, C_K, C_V, C_X, C_C, C_B):
                    load(kview(w[:, bass.ds(h * P + col, P)]), 8, True)
            pos[0] = 0
            for g in range(4):
                load(kview(w[:, C_U + g * P:C_U + (g + 1) * P]), 8)
            with c.trips(4, **turns(12)) as g:
                pos[0] = 0
                for d2 in range(2):
                    at = g * 256 + d2 * P
                    load(kview(w[:, bass.ds(at + C_G, P)]), 8)
                    load(kview(w[:, bass.ds(at + (C_G + D), P)]), 8)
                    load(kview(w_conv_out[l][:, bass.ds(at, P)]), 4, True)
                    load(kview(w_pool[l, bass.ds(g, 1), :, d2 * P:(d2 + 1) * P].rearrange("a c n -> (a c) n")), 1)
                    load(kview(w[:, bass.ds(at + (C_G + 2 * D), P)]), 8)
                    load(kview(w_attn_out[l][:, bass.ds(at, P)]), 4)
            with c.trips(4, **turns(2)) as m2:
                pos[0] = 0
                for j in range(2):
                    load(kview(w_o[l][:, bass.ds(m2 * 256 + j * P, P)]), 8)
            if l == 0:
                with c.trips(2, **both(turns(2, NF), turns(4, 4))) as ch:
                    with c.trips(NF, **turns(2)) as f:
                        pos[0] = 0
                        at = ch * FE + f * P
                        load(kview(w_gate_d[0][:, bass.ds(at, P)]), 8)
                        load(kview(w_up_d[0][:, bass.ds(at, P)]), 8)
                    with c.trips(4, **turns(4)) as m2:
                        pos[0] = 0
                        for k0, k1 in ((0, 8), (8, NF)):
                            for j in range(2):
                                load(kview(w_down_d[0][bass.ds(ch * FE + k0 * P, (k1 - k0) * P),
                                                       bass.ds(m2 * 256 + j * P, P)]), k1 - k0)
            else:
                def expert_tile(j, e):
                    e1 = bass.ds(e, 1) if not isinstance(e, int) else slice(e, e + 1)
                    if j < 2 * NF:
                        w, rs, n0 = (w_gate_e, w_up_e)[j % 2], slice(0, D), j // 2
                    else:
                        m2, q = divmod(j - 2 * NF, 4)
                        w, rs, n0 = w_down_e, (slice(0, D), slice(D, FE))[q // 2], 2 * m2 + q % 2
                    return kview(w[0, e1, rs, n0 * P:(n0 + 1) * P].rearrange("a d n -> (a d) n")), EXPERT_J[j]

                pos[0] = 0
                for j in range(AHEAD_E):
                    load(*expert_tile(j, 0))
                sp.wait_ge(s_go, 1)
                rounds = sp.value_load(rounds_i[0:1, 0:1], min_val=1, max_val=MAXR)
                per = turns(len(EXPERT_J))
                with c.trips(rounds, **{k: NE * v for k, v in per.items()}) as r:
                    with c.trips(NE, **per) as e:
                        pos[0] = AHEAD_E
                        for j in range(AHEAD_E, len(EXPERT_J)):
                            load(*expert_tile(j, e), j >= 2 * NF)
                        for j in [n % NSLOT for n in range(len(EXPERT_J), len(EXPERT_J) + NSLOT)]:
                            pos[0] = j
                            load(*expert_tile(j, (e + 1) % NE), True)

    @block.gpsimd
    def _(pool):
        c = Tallies(pool)

        def squares(before):
            for k in range(KD - 1):
                pool.wait_ge(free[k % 2], before + k // 2 + 2)
                at = SQ + T * k
                pool.tensor_tensor(ar(at, T), xT[:, k, :], xT[:, k, :], ALU.mult).then_inc(s_pool, 1)
                pool.wait_ge(s_pool, c.step.next())
                if k:
                    ins = pool.tensor_tensor(ar(SQ, T), ar(SQ, T), ar(at, T), ALU.add)
                    if k < KD - 2:
                        ins.then_inc(s_pool, 1)
                        pool.wait_ge(s_pool, c.step.next())
            ins.then_inc(s_sq7, 1)

        def odd_lo(norm):
            for k in range(1, KD, 2):
                pool.wait_ge(s_hh, norm * KD + k + 1)
                pool.tensor_tensor(hlo[:, k, :], ar(HF + T * (k % 4), T), hhi[:, k, :].bitcast(F32),
                                   ALU.subtract).then_inc(s_hlo, 1)

        for dst, src in ((R_MIX, norm_mix.rearrange("l (k p) -> (l k) p", p=P)),
                         (R_FFN, norm_ffn.rearrange("l (k p) -> (l k) p", p=P)),
                         (R_PS, pool_scale.rearrange("l (k p) -> (l k) p", p=P)),
                         (R_CW, conv_w.rearrange("l j (k p) -> (l j k) p", p=P)),
                         (R_SUB, subln_g)):
            pool.dma_start(arena[dst:dst + src.shape[0], ROWS:ROWS + P], src).then_inc(s_rows, 16)
        for l in range(DEPTH):
            pool.dma_start(arena[17 * l:17 * l + 2, STROWS:STROWS + 512], state_conv[l, 0]).then_inc(s_state, 16)
            pool.dma_start(arena[17 * l + 2:17 * l + 17, STROWS:STROWS + 512], state_pool[l, 0]).then_inc(s_state, 16)
        for i, a in enumerate((lambda_q1, lambda_k1, lambda_q2, lambda_k2)):
            pool.dma_start(ar(LAMB + P * i, P),
                           a.rearrange("(a l) d -> a (l d)", a=1).partition_broadcast(P)
                           .rearrange("p a n -> p (a n)")).then_inc(s_lam, 16)
        for l in range(DEPTH):
            if l == 0:
                pool.wait_ge(s_kept, NTT)
            else:
                pool.wait_ge(s_xr, 2 * l)
            pool.dma_start(ar(PROB, 512), cache_k[l, 0].rearrange("t h e -> t (h e)")).then_inc(s_cache, 16)
            pool.dma_start(ar(VP, 512), cache_v[l, 0].rearrange("t h e -> t (h e)")).then_inc(s_cache, 16)
            odd_lo(2 * l)
            with c.trips(HEADS, vtok=1, ktok=1) as h:
                h1 = bass.ds(h, 1)
                pool.wait_ge(s_vtok, c.vtok.next() + 1)
                pool.sem_inc(s_pace, 1)
                pool.dma_start(v_prompt[l, 0, :, h1, :].rearrange("(j p) h e -> p j (h e)", p=P),
                               vtok[:, 0:4, :]).then_inc(s_kv, 16)
                pool.dma_start(v_sample[l, 0, :, h1, :].rearrange("t h e -> t (h e)"),
                               vtok[0:TS, 4, :]).then_inc(s_kv, 16)
                pool.wait_ge(s_ktok, c.ktok.next())
                pool.sem_inc(s_pace, 1)
                pool.dma_start(k_prompt[l, 0, :, h1, :].rearrange("(j p) h e -> p j (h e)", p=P),
                               ktok[:, 0:4, :]).then_inc(s_kv, 16)
                pool.dma_start(k_sample[l, 0, :, h1, :].rearrange("t h e -> t (h e)"),
                               ktok[0:TS, 4, :]).then_inc(s_kv, 16)
            pool.wait_ge(s_tk, l + 1)
            for dst, a, b in ((conv_prompt, 0, 2), (conv_sample, 2, 4), (pool_prompt, 4, 19), (pool_sample, 19, 34)):
                pool.dma_start(dst[l, 0], arena[a:b, TROW:TROW + 512]).then_inc(s_ts, 16)
            if l:
                pool.dma_start(WR, kview(w_router[0])).then_inc(s_wr, 16)
                pool.dma_start(BR, b_router.partition_broadcast(P).rearrange("p a n -> p (a n)")).then_inc(s_wr, 16)
            squares(MIX_PAIRS * (l + 1) + FFN_PAIRS * l - 4)
            odd_lo(2 * l + 1)
            if l == 0:
                squares(MIX_PAIRS + FFN_PAIRS - 4)
        pool.wait_ge(s_mix, 1)
        pool.dma_start(ar(GF, D), norm_final.rearrange("(a n) -> a n", a=1).partition_broadcast(P)
                       .rearrange("p a n -> p (a n)")).then_inc(s_gf, 16)
        for j in range(NTT):
            pool.wait_ge(s_fin, j + 1)
            if j < 4:
                pool.dma_start(y_prompt[0, j * P:(j + 1) * P, :], xtok[:, j, :]).then_inc(s_out, 16)
            else:
                pool.dma_start(y_sample[0], xtok[0:TS, 4, :]).then_inc(s_out, 16)
        pool.wait_ge(s_out, 16 * NTT)
        pool.wait_ge(s_kv, 64 * HEADS * DEPTH)
        pool.wait_ge(s_ts, 64 * DEPTH)

    @block.tensor
    def _(pe):
        c = Tallies(pe)
        pos = [0]
        for s in range(NSLOT):
            pe.sem_inc(used[s], 1)
        for p in range(4):
            pe.sem_inc(free[p], 1)

        def product(kt, k0, act_hi, act_lo, p, start=True, stop=True, made=None):
            s = pos[0] % NSLOT
            pos[0] += 1
            if start:
                pe.wait_ge(free[p], c.of("pair", p).next())
            pe.wait_ge(lo_ready[s], c.of("slot", s).next() + 1)
            for k in range(kt):
                if made:
                    pe.wait_ge(*made(k))
                ks = slice(k * P, (k + 1) * P)
                for i, (w, a) in enumerate(((whi, act_hi), (whi, act_lo), (wlo, act_hi))):
                    for q in range(2):
                        mm = pe.matmul(ps[:, 2 * p + q, 0:HALF], w[:, s, ks], a(k0 + k)[:, q * HALF:(q + 1) * HALF],
                                       start=(start and k == 0 and i == 0), stop=(stop and k == kt - 1 and i == 2))
            mm.then_inc(used[s], 1)

        def h_made(norm):
            return lambda k: ((s_hl, s_hlo)[k % 2], norm * KD // 2 + k // 2 + 1)

        def part(j, p, k0, k1):
            s = j % NSLOT
            if k0 == 0:
                pe.wait_ge(free[p], c.of("pair", p).next())
                pe.wait_ge(lo_ready[s], c.of("slot", s).next() + 1)
            for k in range(k0, k1):
                ks = slice(k * P, (k + 1) * P)
                for i, (w, a) in enumerate(((whi, hhi), (whi, hlo), (wlo, hhi))):
                    for q in range(2):
                        mm = pe.matmul(ps[:, 2 * p + q, 0:HALF], w[:, s, ks], a[:, k, q * HALF:(q + 1) * HALF],
                                       start=(k == 0 and i == 0), stop=(k == KD - 1 and i == 2))
            if k1 == KD:
                mm.then_inc(used[s], 1)

        def rows(t, at=0):
            return lambda k: t[:, at + k, :]

        def norm_sums(first=False):
            tiles = [(0, s_sq, 1), (1, s_sq, 2), (2, s_sqp, 1), (4, s_sqp, 2), (6, s_sqp, 3)] if first else \
                    [(0, s_sq7, c.sq7.next()), (7, s_sq, c.sq.next())]
            for n, (k, done, at) in enumerate(tiles):
                pe.wait_ge(done, at)
                for g in range(4):
                    mm = pe.matmul(ps[:, 7, 0:QUARTER], band[:, 96 - 32 * g:224 - 32 * g], ar(SQ + T * k + g * QUARTER, QUARTER),
                                   start=(n == 0 and g == 0), stop=(n == len(tiles) - 1 and g == 3))
            mm.then_inc(s_sum, 1)
            if first:
                c.sq.next(KD)

        def norm_spread():
            pe.wait_ge(s_rcp, c.rcp.next())
            for g in range(4):
                mm = pe.matmul(ps[:, 4 + g // 2, (g % 2) * QUARTER:(g % 2 + 1) * QUARTER],
                               ident[:, 32 * g:32 * g + 1].broadcast_to([P, P]), ar(MS, QUARTER), start=True, stop=True)
            mm.then_inc(s_rin, 1)

        pe.wait_ge(s_ident, 16)
        for j in range(NTT):
            n = P if j < 4 else TS
            pe.wait_ge(s_x[j], 16)
            if j >= 4:
                pe.wait_ge(s_kept, j - 3)
            for k in range(KD):
                mm = pe.transpose(ps[:, 2 * (j % 4) + k // 4, (k % 4) * P:(k % 4) * P + n],
                                  ar(XIN + j * D + k * P, P, n), ident[0:n, 0:n])
            mm.then_inc(s_turned, 1)
        pe.wait_ge(s_rows, 80)
        pe.wait_ge(s_kept, NTT)
        pe.transpose(ps[:, 0, 0:R_N], ar(ROWS, P, R_N), ident[0:R_N, 0:R_N]).then_inc(s_turned, 1)
        pe.wait_ge(s_state, 64)
        for t in range(NC4):
            mm = pe.transpose(ps[:, 1, t * P:t * P + 34], ar(STROWS + t * P, P, 34), ident[0:34, 0:34])
        mm.then_inc(s_turned, 1)
        pe.wait_ge(s_kept, NTT + 2)
        pe.wait_ge(s_ones, 1)
        pe.wait_ge(s_const, 32)

        for l in range(DEPTH):
            norm_sums(l == 0)
            pe.wait_ge(s_cache, 32 * (l + 1))
            for h in range(HEADS):
                mm = pe.transpose(ps[:, 6, h * P:(h + 1) * P], ar(PROB + h * P, P), ident)
            mm.then_inc(s_turned, 1)
            norm_spread()

            with c.trips(HEADS, **turns(6), pair0=3, pair1=3, rope=2, vtok=1, ktok=1, exp=5, a=5, ak=5, ok=5) as h:
                pos[0] = 0
                h1 = bass.ds(h, 1)
                for p in (0, 1, 0):
                    product(8, 0, rows(hhi), rows(hlo), p, made=h_made(2 * l) if pos[0] == 0 else None)
                pe.wait_ge(s_kept, NTT + 3 + l)
                for q in range(2):
                    mm = pe.matmul(ps[:, 4 + q, 0:HALF], kc[:, K_ROT:K_ROT + P], ar(QR + q * HALF, HALF),
                                   start=True, stop=True)
                mm.then_inc(s_rot, 1)
                pe.wait_ge(free[1], c.of("pair", 1).now() + 1)
                pe.wait_ge(s_ok, c.ok.now() + 1)
                for q in range(2):
                    mm = pe.matmul(ps[:, 6 + q, 0:HALF], kc[:, K_ROT:K_ROT + P], ar(KR + q * HALF, HALF),
                                   start=True, stop=True)
                mm.then_inc(s_rot, 1)
                part(3, 1, 0, 2)
                pe.wait_ge(free[0], c.of("pair", 0).now() + 1)
                pe.wait_ge(s_rope, c.rope.next() + 1)
                for j in range(NTT):
                    n = P if j < 4 else TS
                    mm = pe.transpose(ps[0:n, 4 + j // 4, (j % 4) * P:(j % 4 + 1) * P], ar(VR + j * P, n), ident)
                mm.then_inc(s_vt, 1)
                part(3, 1, 2, 4)
                pe.wait_ge(s_rope, c.rope.next() + 1)
                for j in range(NTT):
                    n = P if j < 4 else TS
                    mm = pe.transpose(ps[0:n, 6 + j // 4, (j % 4) * P:(j % 4 + 1) * P], ar(KT + j * P, n), ident)
                mm.then_inc(s_kt, 1)
                pe.wait_ge(s_vtok, c.vtok.next() + 1)

                def scores(u, rq, q0, keys, tiles):
                    if u:
                        pe.wait_ge(s_exp, c.exp.next())
                        pe.sem_inc(s_pace, 1)
                    for cc in range(2):
                        r = slice(64 * cc, 64 * cc + 64)
                        qs = arena[r, QT + q0:QT + q0 + rq]
                        if u < 4:
                            mm = pe.matmul(ps[0:rq, 4 + cc, 0:keys], qs, arena[r, KT:KT + keys], start=True, stop=True)
                        else:
                            pe.matmul(ps[0:rq, 4 + cc, 0:PAST], qs, arena[r, TMP:TMP + PAST], start=True, stop=True)
                            mm = pe.matmul(ps[0:rq, 4 + cc, PAST:keys], qs, arena[r, KT + TP:KT + T],
                                           start=True, stop=True)
                    mm.then_inc(s_sc, 1)

                us = list(units())
                scores(*us[0])
                part(3, 1, 4, 8)
                pe.wait_ge(s_ktok, c.ktok.next())
                for u, rq, q0, keys, tiles in us:
                    if u < 4:
                        scores(*us[u + 1])
                    else:
                        part(5, 1, 6, 8)
                    pe.wait_ge(s_a, c.a.next())
                    pe.sem_inc(s_pace, 1)
                    for j, kn in enumerate(tiles):
                        mm = pe.transpose(ps[0:kn, 6, j * P:j * P + rq], prob[0:rq, 0, j * P:j * P + kn],
                                          ident[0:rq, 0:rq])
                    mm.then_inc(s_at, 1)
                    if u < 4:
                        part(*((4, 0, 0, 4), (4, 0, 4, 8), (5, 1, 0, 4), (5, 1, 4, 6))[u])
                    pe.wait_ge(s_ok, c.ok.next())
                    pe.wait_ge(s_ak, c.ak.next())
                    for j, kn in enumerate(tiles):
                        if u < 4:
                            v = vtok[:, j, :]
                        else:
                            v = vpast[:, h1, :].rearrange("p h e -> p (h e)") if j == 0 else vtok[0:TS, 4, :]
                        mm = pe.matmul(ps[0:rq, 7, 0:P], ar(AT + j * P, rq, kn), v,
                                       start=(j == 0), stop=(j == len(tiles) - 1))
                    mm.then_inc(s_pv, 1)
                c.exp.next()

            pos[0] = 0
            for g in range(4):
                product(8, 0, rows(hhi), rows(hlo), g % 2)
                if g % 2 == 0:
                    continue
                pe.wait_ge(s_on, l + 1)
                pe.wait_ge(s_ok, c.ok.now() + 1)
                for h in (g - 1, g):
                    if h >= 2:
                        pe.wait_ge(s_ol, 4 * l + h - 1)
                    b = 4 + 2 * (h % 2)
                    for j in range(NTT):
                        n = P if j < 4 else TS
                        mm = pe.transpose(ps[:, b + j // 4, (j % 4) * P:(j % 4) * P + n], oq[0:n, j, h, :],
                                          ident[0:n, 0:n])
                    mm.then_inc(s_ot, 1)

            with c.trips(4, **turns(12), pair0=6, pair1=6) as g:
                pos[0] = 0
                g4 = bass.ds(g + 4, 1)
                for d2 in range(2):
                    product(8, 0, rows(hhi), rows(hlo), 0)
                    product(8, 0, rows(hhi), rows(hlo), 1)
                    pe.wait_ge(s_bl, 8 * l + 4 + 1)
                    product(4, 0, rows(bhi), rows(blo), 0)
                    pe.wait_ge(s_bl, 8 * l + 8 + 1)
                    product(1, 0, lambda k: bhi[:, g4, :].rearrange("p a t -> p (a t)"),
                            lambda k: blo[:, g4, :].rearrange("p a t -> p (a t)"), 1)
                    product(8, 0, rows(hhi), rows(hlo), 0)
                    pe.wait_ge(s_ol, 4 * l + 4)
                    product(4, 0, rows(bhi, 8), rows(blo, 8), 1)

            for t in range(NC4):
                mm = pe.transpose(ps[0:34, 6, t * P:(t + 1) * P], tails[:, t, :], ident)
            mm.then_inc(s_tt, 1)
            with c.trips(4, **turns(2), pair0=1, pair1=1):
                pos[0] = 0
                for j in range(2):
                    product(8, 0, rows(bhi), rows(blo), j, made=(lambda k: (s_ml, l * KD + k + 1)) if j == 0 else None)
            norm_sums()
            norm_spread()
            if l == 0:
                with c.trips(2, **both(turns(2, NF), turns(4, 4)), pair0=NF + 4, pair1=NF + 4, fl=NF):
                    with c.trips(NF, **turns(2), pair0=1, pair1=1):
                        pos[0] = 0
                        product(8, 0, rows(hhi), rows(hlo), 0, made=h_made(1))
                        product(8, 0, rows(hhi), rows(hlo), 1)
                    with c.trips(4, **turns(4), pair0=1, pair1=1):
                        pos[0] = 0
                        for k0, k1 in ((0, 8), (8, NF)):
                            pe.wait_ge(s_fl, c.fl.now() + k1)
                            pe.sem_inc(s_pace, 1)
                            for j in range(2):
                                product(k1 - k0, k0, rows(bhi), rows(blo), j, k0 == 0, k1 == NF)
                    c.fl.next(NF)

        pe.wait_ge(s_rw, 2)
        for k in range(KD):
            pe.wait_ge(*h_made(2 * DEPTH - 1)(k))
            for i, (a, w) in enumerate(((hhi, 0), (hlo, 0), (hhi, 1))):
                for q in range(2):
                    mm = pe.matmul(ps[0:NE, q, 0:HALF], selr[:, w * 64 + k * NE:w * 64 + (k + 1) * NE],
                                   a[:, k, q * HALF:(q + 1) * HALF],
                                   start=(k == 0 and i == 0), stop=(k == KD - 1 and i == 2))
        mm.then_inc(s_lge, 1)
        def positions():
            pe.wait_ge(s_rt, 1)
            for j in range(NTT):
                n = P if j < 4 else TS
                for i in range(j + 1):
                    kn = P if i < 4 else TS
                    mm = pe.matmul(ps[0:n, 6, 8 * j:8 * j + 8], (kc[0:kn, K_TRI:K_TRI + n] if i == j else ones[0:kn, 0:n]),
                                   RM[0:kn, i, :], start=(i == 0), stop=(i == j))
            for i in range(NTT):
                kn = P if i < 4 else TS
                mm = pe.matmul(ps[:, 7, 0:8], ones[0:kn, :], RM[0:kn, i, :], start=(i == 0), stop=(i == NTT - 1))
            mm.then_inc(s_pos, 1)

        n_t = 0
        for j in range(NTT):
            n = P if j < 4 else TS
            for src in (hhi, hlo, xT):
                for g in range(2):
                    b = 2 + n_t % 4
                    if n_t >= 4:
                        pe.wait_ge(s_hk, sum(1 for i in range(n_t - 3) if i % 6 < 4))
                        if any(i % 6 >= 4 for i in range(n_t - 3)):
                            pe.wait_ge(s_hkd, sum(1 for i in range(n_t - 3) if i % 6 >= 4))
                    for k in range(4):
                        v = src[:, 4 * g + k, j * P:j * P + n]
                        if src is not xT:
                            v = v.bitcast(F32)
                        mm = pe.transpose(ps[0:n, b, k * P:(k + 1) * P], v, ident)
                    mm.then_inc(s_ht, 1)
                    n_t += 1
            if j == 0:
                pe.wait_ge(s_lgk, 1)
                for i in range(NTT):
                    n = P if i < 4 else TS
                    mm = pe.transpose(ps[0:n, 0, NE * i:NE * (i + 1)], LGT[:, i * P:i * P + n], ident[0:NE, 0:NE])
                mm.then_inc(s_lg, 1)
            if j == 2:
                positions()
        pe.wait_ge(s_hk, 20)
        pe.wait_ge(s_hkd, 10)
        pe.wait_ge(s_go, 1)
        rounds = pe.value_load(rounds_i[0:1, 0:1], min_val=1, max_val=MAXR)
        per = both(turns(len(EXPERT_J)), dict(pair0=6 + 4, pair1=6 + 4, pair2=5, pair3=5, sel=1, gl=8, stk=1,
                                              fl=NF, yl=4, acc=10))

        def product_e(kt, k0, a, b, start=True, stop=True):
            s = pos[0] % NSLOT
            pos[0] += 1
            if start:
                pe.wait_ge(free[b], c.of("pair", b).next())
            pe.wait_ge(lo_ready[s], c.of("slot", s).next() + 1)
            for k in range(kt):
                ks = slice(k * P, (k + 1) * P)
                first, last = start and k == 0, stop and k == kt - 1
                if not last:
                    pe.matmul(ps[:, b, 0:2 * CAP].rearrange("p (i c) -> p i c", i=2), whi[:, s, ks],
                              a[:, :, k0 + k, :], start=first, stop=False)
                mm = pe.matmul(ps[:, b, CAP:2 * CAP], wlo[:, s, ks], a[:, 0, k0 + k, :], start=False, stop=False)
                if last:
                    mm = pe.matmul(ps[:, b, 0:2 * CAP].rearrange("p (i c) -> p i c", i=2), whi[:, s, ks],
                                   a[:, :, k0 + k, :], start=False, stop=True)
            mm.then_inc(used[s], 1)

        with c.trips(rounds, **{k: NE * v for k, v in per.items()}):
            with c.trips(NE, **per):
                pos[0] = 0
                pe.wait_ge(s_sel, c.sel.next())
                for d in range(KD):
                    if d < 4:
                        pe.wait_ge(s_acc, c.acc.now() + 1 + d)
                    if d >= 4:
                        pe.wait_ge(s_gl, c.gl.now() + d - 3)
                    for j in range(NTT):
                        kn = P if j < 4 else TS
                        for i in range(2):
                            mm = pe.matmul(ps[:, GATHER[d % 4], 0:CAP], htok[i][0:kn, j, d * P:(d + 1) * P],
                                           sel[0:kn, j, :], start=(j == 0 and i == 0), stop=(j == NTT - 1 and i == 1))
                    mm.then_inc(s_ga, 1)
                for a, cn in enumerate(CAPT):
                    pe.wait_ge(s_gl, c.gl.now() + 7 + a)
                    pe.sem_inc(s_pace, 1)
                    for j in range(NTT):
                        kn = P if j < 4 else TS
                        mm = pe.transpose(ps[0:cn, 4 + 2 * a + j // 4, (j % 4) * P:(j % 4) * P + kn],
                                          sel[0:kn, j, a * P:a * P + cn].bitcast(F32), ident[0:kn, 0:kn])
                mm.then_inc(s_st, 1)
                c.gl.next(8)
                for f in range(NF):
                    product_e(8, 0, hg, 2 * (f % 2))
                    product_e(8, 0, hg, 2 * (f % 2) + 1)
                for m2 in range(4):
                    for k0, k1 in ((0, 8), (8, NF)):
                        if m2 == 0:
                            pe.wait_ge(s_fl, c.fl.now() + k1)
                            pe.sem_inc(s_pace, 1)
                        for j in range(2):
                            product_e(k1 - k0, k0, ea, j, k0 == 0, k1 == NF)
                c.fl.next(NF)
                pe.wait_ge(s_stk, c.stk.next())
                pe.sem_inc(s_pace, 1)
                for g in range(2):
                    for q in range(2):
                        pe.wait_ge(free[q], c.of("pair", q).now() + (1 if g else -1))
                        pe.sem_inc(s_pace, 1)
                    for a, cn in enumerate(CAPT):
                        for k in range(4):
                            mm = pe.transpose(ps[0:cn, 4 + 2 * a + g, k * P:(k + 1) * P],
                                              yT[:, 4 * g + k, a * P:a * P + cn], ident)
                        mm.then_inc(s_yt, 1)
                for n in range(2 * NTT):
                    g, j = divmod(n, NTT)
                    rows_ = P if j < 4 else TS
                    if n in (0, 2):
                        pe.wait_ge(s_yl, c.yl.now() + 2 + n)
                        pe.sem_inc(s_pace, 1)
                    if n >= 4:
                        pe.wait_ge(s_acc, c.acc.now() + 4 + n - 3)
                    for a, cn in enumerate(CAPT):
                        for i in range(2):
                            mm = pe.matmul(ps[0:rows_, SPREAD[n % 4], 0:512], selT[0:cn, a, j * P:j * P + rows_],
                                           ey[0:cn, i, a, g * 512:(g + 1) * 512],
                                           start=(a == 0 and i == 0), stop=(a == 1 and i == 1))
                    mm.then_inc(s_sp, 1)
                c.yl.next(4)
                c.acc.next(10)

    @block.scalar
    def _(act):
        c = Tallies(act)
        pos = [0]

        def split(js, p):
            kt = js[p] if p < len(js) else 8
            s = (p if p < len(js) else p - len(js)) % NSLOT
            n = c.of("slot", s).next()
            act.wait_ge(landed[s], n * 16)
            act.wait_ge(used[s], n)
            act.activation(whi[:, s, 0:kt * P], raw[:, s, 0:kt * P], ACT.Copy).then_inc(hi_ready[s], 1)

        def ready(j):
            n = c.of("seen", j % NSLOT).next()
            act.wait_ge(used[j % NSLOT], n + 1)

        def skip(j):
            c.of("seen", j % NSLOT).next()

        def seen(n, times=1):
            return {k.replace("slot", "seen"): v for k, v in turns(n, times).items()}

        def norm_act(first=False):
            if first:
                for k in range(KD):
                    act.activation(ar(SQ + T * k, T), xT[:, k, :], ACT.Square).then_inc(s_sq, 1)
            else:
                act.wait_ge(free[1], c.of("pair", 1).now() + 1)
                act.activation(ar(SQ + T * (KD - 1), T), xT[:, KD - 1, :], ACT.Square).then_inc(s_sq, 1)
            act.activation(small[0:1, 63:64], ones[0:1, 0:1], ACT.Sqrt)
            act.wait_ge(s_ms, c.ms.next())
            act.activation(ar(MS, QUARTER), ar(MS, QUARTER), ACT.Sqrt).then_inc(s_rms, 1)
            for k in range(KD):
                act.wait_ge(s_hf, c.hf.next())
                act.activation(hhi[:, k, :], ar(HF + T * (k % 4), T), ACT.Copy).then_inc(s_hh, 1)

        act.wait_ge(s_lamp, 1)
        act.activation(lam4, lam4, ACT.Exp).then_inc(s_lame, 1)
        for s in range(AHEAD):
            split([8, 8], s)
        act.wait_ge(s_kept, NTT + 2)

        for l in range(DEPTH):
            norm_act(l == 0)
            with c.trips(HEADS, **turns(6), **seen(6), pair0=3, pair1=3, rope=2, vtok=1, mx=5, at=5, bl=1) as h:
                h1 = bass.ds(h, 1)
                for j, dst in enumerate((QR, KR, VR)):
                    split(HEAD_J, j + 2)
                    if j == 2:
                        split(HEAD_J, 5)
                    ready(j)
                    if j < 2:
                        act.wait_ge(s_rope, c.rope.now() + 1)
                    else:
                        act.wait_ge(s_vtok, c.vtok.now() + 1)
                    act.activation(halves(ar(dst, T)), bank2(j % 2), ACT.Copy).then_inc(free[j % 2], 1)
                    c.of("pair", j % 2).next()
                for u, rq, q0, keys, tiles in units():
                    act.wait_ge(s_mx, c.mx.next())
                    if u:
                        act.wait_ge(s_at, c.at.next())
                    for cc in range(2):
                        mm = act.activation(prob[0:rq, cc, 0:keys], ps[0:rq, 4 + cc, 0:keys], ACT.Exp,
                                            bias=nbias[0:rq, cc:cc + 1], scale=SCALE,
                                            accum_out=psum2[0:rq, cc:cc + 1])
                    mm.then_inc(s_exp, 1)
                    if u == 0:
                        ready(3)
                        act.wait_ge(s_bl, c.bl.next() + 4 * l)
                        act.activation(halves(xs), bank2(1), ACT.Copy).then_inc(free[1], 1)
                        c.of("pair", 1).next()
                    elif u == 2:
                        split(HEAD_J, 6)
                        skip(4)
                        c.of("pair", 0).next()
                split(HEAD_J, 7)
                skip(5)
                act.wait_ge(free[1], c.of("pair", 1).next() + 1)
                act.activation(bhi[:, h1, :].rearrange("p a t -> p (a t)"), xs, ACT.Copy).then_inc(s_bh, 1)
                c.at.next()
                c.rope.next(2)
                c.vtok.next()
            act.wait_ge(s_ok, 20 * (l + 1) + 1)
            for b in range(NTT):
                n = P if b < 4 else TS
                for h in range(HEADS):
                    mm = act.activation(ar(VR, P, n), oq[0:n, b, h, :], ACT.Square,
                                        accum_out=osum[0:n, 4 * b + h:4 * b + h + 1])
                    mm.then_inc(s_act, 1)
                    act.wait_ge(s_act, c.act.next())
            act.drain().then_inc(s_osq, 1)
            act.wait_ge(s_ms, c.ms.next())
            act.activation(orms, orms, ACT.Sqrt).then_inc(s_rms, 1)

            for g in range(4):
                split(POOL_J, g + 2)
                ready(g)
                act.wait_ge(s_pad, c.pad.next())
                at = UX + 576 * (g % 2)
                p = g % 2
                act.activation(ar(at + HIST, HALF), ps[:, 2 * p, 0:HALF], ACT.Copy)
                act.activation(ar(at + HIST + HALF, TP - HALF), ps[:, 2 * p + 1, 0:TP - HALF], ACT.Copy)
                act.activation(ar(at + 2 * HIST + TP, TS), ps[:, 2 * p + 1, TP - HALF:HALF],
                               ACT.Copy).then_inc(free[p], 1)
                c.of("pair", p).next()
                act.wait_ge(s_by, c.by.next())
                act.activation(bhi[:, 4 + g, 0:TP], ar(PM + HIST, TP), ACT.Copy)
                act.activation(bhi[:, 4 + g, TP:T], ar(PM + 2 * HIST + TP, TS), ACT.Copy).then_inc(s_bh, 1)
                if g % 2 == 0:
                    continue
                for h in (g - 1, g):
                    act.wait_ge(s_ot, c.ot.next())
                    b = 4 + 2 * (h % 2)
                    act.activation(bhi[:, 8 + h, 0:TP], ps[:, b, 0:TP], ACT.Copy, scale=par[:, R_SUB + l:R_SUB + l + 1])
                    act.activation(bhi[:, 8 + h, TP:T], ps[:, b + 1, 0:TS], ACT.Copy,
                                   scale=par[:, R_SUB + l:R_SUB + l + 1]).then_inc(s_oh, 1)
            with c.trips(4, **turns(12), **seen(12), pair0=6, pair1=6):
                for d2 in range(2):
                    for j, dst, p in ((0, SA, 0), (1, SB_, 1), (2, None, 0), (3, None, 1), (4, SC_, 0), (5, None, 1)):
                        split(GATE_J, 6 * d2 + j + 2)
                        c.of("pair", p).next()
                        if dst is None:
                            skip(6 * d2 + j)
                            continue
                        ready(6 * d2 + j)
                        act.activation(halves(ar(dst, T)), bank2(p), ACT.Sigmoid).then_inc(free[p], 1)
            for k in range(KD):
                act.wait_ge(s_mg, l * KD + k + 1)
                act.activation(bhi[:, k, :], mrg[:, k, :], ACT.Copy).then_inc(s_mh, 1)
            with c.trips(4, **turns(2), **seen(2), pair0=1, pair1=1):
                for j in range(2):
                    split(OUT_J, j + 2)
                    skip(j)
                    c.of("pair", j).next()
            if l:
                act.wait_ge(s_wr, 32)
                act.activation(selr[:, 0:64], WR.rearrange("p k e -> p (k e)"), ACT.Copy).then_inc(s_rw, 1)
            norm_act()
            if l == 0:
                with c.trips(2, **both(turns(2, NF), turns(4, 4), seen(2, NF), seen(4, 4)), pair0=NF + 4,
                             pair1=NF + 4):
                    with c.trips(NF, **turns(2), **seen(2), pair0=1, pair1=1) as f:
                        split(UP_J, 2)
                        ready(0)
                        act.activation(halves(ar(FS, T)), bank2(0), ACT.Silu).then_inc(free[0], 1)
                        split(UP_J, 3)
                        skip(1)
                        c.of("pair", 0).next()
                        act.wait_ge(free[1], c.of("pair", 1).next() + 1)
                        act.activation(bhi[:, bass.ds(f, 1), :].rearrange("p a t -> p (a t)"), ar(FA, T),
                                       ACT.Copy).then_inc(s_fh, 1)
                    with c.trips(4, **turns(4), **seen(4), pair0=1, pair1=1):
                        for j in range(4):
                            split(DOWN_J, j + 2)
                            skip(j)
                            if j >= 2:
                                c.of("pair", j - 2).next()

        for p in range(AHEAD, AHEAD_E):
            split(EXPERT_J, p)
        for j in range(NTT):
            n = P if j < 4 else TS
            for i in range(2):
                for g in range(2):
                    t = 6 * j + 2 * i + g
                    act.wait_ge(s_ht, t + 1)
                    act.activation(htok[i][0:n, j, g * 512:(g + 1) * 512], ps[0:n, 2 + t % 4, :],
                                   ACT.Copy).then_inc(s_hk, 1)
            if j == 1:
                act.wait_ge(s_re, 1)
                act.activation(R1[2], R1[2], ACT.Exp).then_inc(s_rx, 1)
        act.wait_ge(s_go, 1)
        rounds = act.value_load(rounds_i[0:1, 0:1], min_val=1, max_val=MAXR)
        per = both(turns(len(EXPERT_J)), seen(len(EXPERT_J)), dict(ga=8, st=1, yt=4, em=NF, pair0=10, pair1=10, pair2=5, pair3=5))

        def hidden_hi(f):
            act.wait_ge(s_em, c.em.next())
            act.activation(ea[:, 0, f, :], ar(EA + CAP * (f % 2), CAP), ACT.Copy).then_inc(s_fh, 1)

        with c.trips(rounds, **{k: NE * v for k, v in per.items()}):
            with c.trips(NE, **per):
                for d in range(KD):
                    act.wait_ge(s_ga, c.ga.next())
                    act.activation(hg[:, 0, d, :], ps[:, GATHER[d % 4], 0:CAP], ACT.Copy).then_inc(s_gh, 1)
                act.wait_ge(s_st, c.st.next())
                for a, cn in enumerate(CAPT):
                    act.activation(selT[0:cn, a, 0:TP], ps[0:cn, 4 + 2 * a, :], ACT.Copy)
                    last = act.activation(selT[0:cn, a, TP:T], ps[0:cn, 5 + 2 * a, 0:TS], ACT.Copy)
                last.then_inc(s_stk, 1)
                for f in range(NF):
                    skip(2 * f)
                    split(EXPERT_J, 2 * f + AHEAD_E)
                    act.wait_ge(free[2 * (f % 2)], c.of("pair", 2 * (f % 2)).next() + 1)
                    act.activation(ar(ES + CAP * (f % 2), CAP), ar(ES + CAP * (f % 2), CAP), ACT.Silu).then_inc(s_si, 1)
                    if f:
                        hidden_hi(f - 1)
                    split(EXPERT_J, 2 * f + 1 + AHEAD_E)
                    skip(2 * f + 1)
                    c.of("pair", 2 * (f % 2) + 1).next()
                hidden_hi(NF - 1)
                for m2 in range(4):
                    for q in range(4):
                        j = 2 * NF + 4 * m2 + q
                        if m2 < 3 or q < 2:
                            split(EXPERT_J, refill(j))
                        skip(j)
                        if q >= 2:
                            c.of("pair", q - 2).next()
                for g in range(2):
                    for a, cn in enumerate(CAPT):
                        act.wait_ge(s_yt, c.yt.next())
                        act.activation(ey[0:cn, 0, a, g * 512:(g + 1) * 512], ps[0:cn, 4 + 2 * a + g, :],
                                       ACT.Copy).then_inc(s_yh, 1)
                for j in (-2, -1):
                    split(EXPERT_J, refill(len(EXPERT_J) + j))
        act.wait_ge(s_mix, 1)
        for j in range(NTT):
            n = P if j < 4 else TS
            act.activation(ar(EA, D, n), xtok[0:n, j, :], ACT.Square, accum_out=fsum[0:n, j:j + 1]).then_inc(s_act, 1)
            act.wait_ge(s_act, c.act.next())
        act.drain().then_inc(s_fsq, 1)
        act.wait_ge(s_ms, c.ms.next())
        act.activation(frms, frms, ACT.Sqrt).then_inc(s_frm, 1)

    @block.vector
    def _(dve):
        c = Tallies(dve)

        def step(ins):
            ins.then_inc(s_dve, 1)
            dve.wait_ge(s_dve, c.step.next())

        def split(js, p):
            kt = js[p] if p < len(js) else 8
            s = (p if p < len(js) else p - len(js)) % NSLOT
            dve.wait_ge(hi_ready[s], c.of("slot", s).next())
            dve.tensor_tensor(wlo[:, s, 0:kt * P], raw[:, s, 0:kt * P], whi[:, s, 0:kt * P].bitcast(F32),
                              ALU.subtract).then_inc(lo_ready[s], 1)

        def ready(j):
            dve.wait_ge(used[j % NSLOT], c.of("seen", j % NSLOT).next() + 1)

        def skip(j):
            c.of("seen", j % NSLOT).next()

        def seen(n, times=1):
            return {k.replace("slot", "seen"): v for k, v in turns(n, times).items()}

        def norm_dve(gain, cache=None, first=False):
            if first:
                for k in (2, 4, 6):
                    dve.wait_ge(s_sq, k + 2)
                    dve.tensor_tensor(ar(SQ + T * k, T), ar(SQ + T * k, T), ar(SQ + T * k + T, T),
                                      ALU.add).then_inc(s_sqp, 1)
            dve.wait_ge(s_sum, c.sum.next())
            dve.tensor_scalar(ar(MS, QUARTER), ps[:, 7, 0:QUARTER], 1.0 / D, EPS, ALU.mult, ALU.add).then_inc(s_ms, 1)
            if cache is not None:
                dve.wait_ge(s_turned, NTT + 3 + cache)
                dve.tensor_copy(kpT, ps[:, 6, :].rearrange("p (h t) -> p h t", h=HEADS)).then_inc(s_kept, 1)
            dve.wait_ge(s_rms, c.rms.next())
            dve.reciprocal(ar(MS, QUARTER), ar(MS, QUARTER)).then_inc(s_rcp, 1)
            dve.wait_ge(s_rin, c.rin.next())

            def full(k):
                if k >= 4:
                    dve.wait_ge(*((s_hl, c.hl.now() + k // 2 - 1), (s_hlo, c.hlo.now() + k // 2 - 1))[k % 2])
                dve.scalar_tensor_tensor(out=halves(ar(HF + T * (k % 4), T)), in0=halves(xT[:, k, :]),
                                         scalar=par[:, gain + k:gain + k + 1], in1=ps[:, 4:6, 0:HALF],
                                         op0=ALU.mult, op1=ALU.mult).then_inc(s_hf, 1)

            full(0)
            for k in range(0, KD, 2):
                full(k + 1)
                if k + 2 < KD:
                    full(k + 2)
                dve.wait_ge(s_hh, c.hh.now() + k + 1)
                dve.tensor_tensor(hlo[:, k, :], ar(HF + T * (k % 4), T), hhi[:, k, :].bitcast(F32),
                                  ALU.subtract).then_inc(s_hl, 1)
            c.hh.next(KD)
            c.hl.next(KD // 2)
            c.hlo.next(KD // 2)

        for s in range(NSLOT):
            dve.sem_inc(lo_ready[s], 1)
        dve.sem_inc(s_rope, 1)
        dve.sem_inc(s_vtok, 1)
        dve.sem_inc(s_ok, 1)
        dve.sem_inc(s_acc, 4)
        dve.sem_inc(s_bl, 1)
        step(dve.memset(band[:], 0.0))
        dve.memset(band[:, 96:P], 1.0)
        dve.memset(ones[:], 1.0).then_inc(s_ones, 1)
        step(dve.memset(small[:], 1.0))
        for j in range(NTT):
            n = P if j < 4 else TS
            dve.wait_ge(s_turned, j + 1)
            for g in range(2):
                ins = dve.tensor_copy(xT[:, 4 * g:4 * g + 4, j * P:j * P + n],
                                      ps[:, 2 * (j % 4) + g, :].rearrange("p (k t) -> p k t", k=4)[:, :, 0:n])
            ins.then_inc(s_kept, 1)
        dve.wait_ge(s_turned, NTT + 1)
        dve.tensor_copy(par[:], ps[:, 0, 0:R_N]).then_inc(s_kept, 1)
        dve.wait_ge(s_turned, NTT + 2)
        dve.tensor_copy(stT[:], ps[:, 1, :].rearrange("p (t n) -> p t n", t=NC4)[:, :, 0:34]).then_inc(s_kept, 1)
        dve.wait_ge(s_lam, 64)
        for i in range(2):
            step(dve.tensor_tensor(ar(LAMB + 2 * P * i, P), ar(LAMB + 2 * P * i, P), ar(LAMB + 2 * P * i + P, P), ALU.mult))
            ins = dve.tensor_reduce(lam4[:, 2 * i:2 * i + 2], ar(LAMB + 2 * P * i, P).rearrange("p (l d) -> p l d", l=2),
                                    AX, ALU.add)
            if i == 0:
                step(ins)
        ins.then_inc(s_lamp, 1)
        dve.wait_ge(s_lame, 1)
        step(dve.tensor_tensor(neglam, lam4[:, 2:4], lam4[:, 0:2], ALU.subtract))
        for l in range(DEPTH):
            step(dve.tensor_scalar(neglam[:, l:l + 1], neglam[:, l:l + 1], lam_init(l), None, ALU.subtract))
        for s in range(AHEAD):
            split([8, 8], s)
        dve.wait_ge(s_kept, NTT + 2)
        dve.wait_ge(s_const, 32)

        for l in range(DEPTH):
            norm_dve(R_MIX + 8 * l, l, l == 0)

            with c.trips(HEADS, **turns(6), **seen(6), pair0=3, pair1=3, rot=2, vt=1, kt=1, kv=64, sc=5, exp=5, at=5,
                         pv=5, step=29, rope=2, bh=1, bl=1) as h:
                h1 = bass.ds(h, 1)
                for j in range(4):
                    split(HEAD_J, j + 2)
                    skip(j)
                    c.of("pair", j % 2).next()
                for src, dst, b in ((QR, QT, 4), (KR, KT, 6)):
                    dve.wait_ge(s_rot, c.rot.next())
                    dve.tensor_tensor(ar(dst, T), ar(src, T), kc[:, K_COS:K_COS + T], ALU.mult)
                    step(dve.tensor_tensor(halves(ar(TMP, T)), ps[:, b:b + 2, 0:HALF],
                                           halves(kc[:, K_SIN:K_SIN + T]), ALU.mult))
                    dve.tensor_tensor(ar(dst, T), ar(dst, T), ar(TMP, T), ALU.add).then_inc(s_rope, 1)
                    dve.wait_ge(s_rope, c.rope.next() + 1)
                dve.tensor_copy(ar(TMP, PAST), kpT[:, bass.ds(h, 1), :].rearrange("p h t -> p (h t)"))
                dve.wait_ge(s_vt, c.vt.next())
                dve.tensor_copy(vtok[:, 0:4, :], ps[:, 4, :].rearrange("p (j e) -> p j e", j=4))
                dve.tensor_copy(vtok[0:TS, 4, :], ps[0:TS, 5, 0:P]).then_inc(s_vtok, 1)
                dve.wait_ge(s_kt, c.kt.next())
                dve.tensor_copy(ktok[:, 0:4, :], ps[:, 6, :].rearrange("p (j e) -> p j e", j=4))
                dve.tensor_copy(ktok[0:TS, 4, :], ps[0:TS, 7, 0:P]).then_inc(s_ktok, 1)

                def maxima(u, rq, q0, keys, tiles):
                    dve.wait_ge(s_sc, c.sc.next())
                    if u < 4:
                        step(dve.memset(ps[0:64, 4:6, keys - 64:keys], NEG))
                    step(dve.tensor_reduce(smax[0:rq, :], ps[0:rq, 4:6, 0:keys], AX, ALU.max))
                    dve.tensor_scalar(nbias[0:rq, :], smax[0:rq, :], -SCALE, None, ALU.mult).then_inc(s_mx, 1)

                us = list(units())
                maxima(*us[0])
                for u, rq, q0, keys, tiles in us:
                    dve.wait_ge(s_exp, c.exp.next())
                    step(dve.reciprocal(prcp[0:rq, :], psum2[0:rq, :]))
                    step(dve.tensor_tensor(prcp[0:rq, 1:2], prcp[0:rq, 1:2], neglam[0:rq, l:l + 1], ALU.mult))
                    step(dve.tensor_scalar(prob[0:rq, 0, 0:keys], prob[0:rq, 0, 0:keys], prcp[0:rq, 0:1], None, ALU.mult))
                    dve.scalar_tensor_tensor(out=prob[0:rq, 0, 0:keys], in0=prob[0:rq, 1, 0:keys],
                                             scalar=prcp[0:rq, 1:2], in1=prob[0:rq, 0, 0:keys],
                                             op0=ALU.mult, op1=ALU.add).then_inc(s_a, 1)
                    if u < 4:
                        maxima(*us[u + 1])
                    dve.wait_ge(s_at, c.at.next())
                    if u < 4:
                        dve.tensor_copy(ar(AT, keys), ps[:, 6, 0:keys]).then_inc(s_ak, 1)
                    else:
                        dve.tensor_copy(ar(AT, TS), ps[:, 6, 0:TS])
                        dve.tensor_copy(ar(AT + P, TS, TS), ps[0:TS, 6, P:P + TS]).then_inc(s_ak, 1)
                    if u == 2:
                        ready(4)
                        dve.wait_ge(free[1], c.of("pair", 1).now() + 1)
                        dve.memset(ext[:, 0:2], 0.0)
                        dve.tensor_copy(ext[:, TP + 2:TP + 4],
                                        stT[:, h1, 17 * l:17 * l + 2].rearrange("p a n -> p (a n)"))
                        dve.tensor_tensor(ext[:, 2:2 + HALF], ps[:, 0, 0:HALF], xs[:, 0:HALF], ALU.mult)
                        dve.tensor_tensor(ext[:, 2 + HALF:2 + TP], ps[:, 1, 0:TP - HALF], xs[:, HALF:TP], ALU.mult)
                        dve.tensor_tensor(ext[:, TP + 4:], ps[:, 1, TP - HALF:HALF], xs[:, TP:T], ALU.mult)\
                           .then_inc(free[0], 1)
                        dve.wait_ge(free[0], c.of("pair", 0).next() + 1)
                        dve.tensor_copy(tails[:, h1, 0:2].rearrange("p a n -> p (a n)"), ext[:, TP:TP + 2])
                        dve.tensor_copy(tails[:, h1, 2:4].rearrange("p a n -> p (a n)"), ext[:, T + 2:T + 4])
                        split(HEAD_J, 6)
                    elif u == 3:
                        def wj(j):
                            return par[:, bass.ds(h + (R_CW + 12 * l + 4 * j), 1)]
                        step(dve.tensor_scalar(cv, ext[:, 0:T + 2], wj(0), None, ALU.mult))
                        for j in (1, 2):
                            step(dve.scalar_tensor_tensor(out=cv, in0=ext[:, j:T + 2 + j], scalar=wj(j),
                                                          in1=cv, op0=ALU.mult, op1=ALU.add))
                    dve.wait_ge(s_pv, c.pv.next())
                    dve.tensor_copy(oq[0:rq, u, bass.ds(h, 1), :].rearrange("p h e -> p (h e)"),
                                    ps[0:rq, 7, 0:P]).then_inc(s_ok, 1)
                ready(5)
                dve.tensor_tensor(xs[:, 0:HALF], ps[:, 2, 0:HALF], cv[:, 0:HALF], ALU.mult)
                dve.tensor_tensor(xs[:, HALF:TP], ps[:, 3, 0:TP - HALF], cv[:, HALF:TP], ALU.mult)
                dve.tensor_tensor(xs[:, TP:T], ps[:, 3, TP - HALF:HALF], cv[:, TP + 2:T + 2], ALU.mult)\
                   .then_inc(free[1], 1)
                c.of("pair", 1).next()
                split(HEAD_J, 7)
                dve.wait_ge(s_bh, c.bh.next())
                dve.tensor_tensor(blo[:, h1, :].rearrange("p a t -> p (a t)"), xs,
                                  bhi[:, h1, :].rearrange("p a t -> p (a t)").bitcast(F32),
                                  ALU.subtract).then_inc(s_bl, 1)
                dve.wait_ge(s_bl, c.bl.next() + 1)
                dve.wait_ge(s_kv, c.kv.next(64))

            dve.wait_ge(s_osq, l + 1)
            dve.tensor_scalar(orms, osum, 1.0 / P, SUB_EPS, ALU.mult, ALU.add).then_inc(s_ms, 1)
            dve.wait_ge(s_rms, c.rms.next())
            step(dve.reciprocal(orms, orms))
            step(dve.tensor_scalar(orms, orms, 1.0 - lam_init(l), None, ALU.mult))
            for b in range(NTT):
                n = P if b < 4 else TS
                last = dve.tensor_tensor(oq[0:n, b, :, :], oq[0:n, b, :, :],
                                         orms[0:n, 4 * b:4 * b + 4].rearrange("p (h a) -> p h a", a=1)
                                         .broadcast_to([n, HEADS, P]), ALU.mult)
            last.then_inc(s_on, 1)

            for g in range(4):
                at = UX + 576 * (g % 2)
                dve.memset(ar(at, HIST), 0.0)
                dve.tensor_copy(ar(at + HIST + TP, HIST), stT[:, g, 17 * l + 2:17 * l + 17]).then_inc(s_pad, 1)
                split(POOL_J, g + 2)
                skip(g)
                p = g % 2
                c.of("pair", p).next()
                dve.wait_ge(free[p], c.of("pair", p).now() + 1)
                dve.tensor_copy(tails[:, g, 4:19], ar(at + TP, HIST))
                dve.tensor_copy(tails[:, g, 19:34], ar(at + TP + HIST + TS, HIST))
                n, lag, src = 574, 1, at
                for i in range(g + 1):
                    dst = (PA, PB)[i % 2]
                    first = 2 * lag - 1
                    step(dve.tensor_tensor(ar(dst + first, n - first), ar(src + first, n - first),
                                           ar(src + first - lag, n - first), ALU.add))
                    src, lag = dst, 2 * lag
                step(dve.scalar_tensor_tensor(out=ar(PM + HIST, n - HIST), in0=ar(src + HIST, n - HIST),
                                              scalar=1.0 / lag, in1=ar(at + HIST, n - HIST),
                                              op0=ALU.mult, op1=ALU.subtract))
                step(dve.tensor_tensor(ar(PM + HIST, HIST), ar(src + HIST, HIST),
                                       kc[:, K_RC + HIST * g:K_RC + HIST * (g + 1)], ALU.mult))
                dve.tensor_tensor(ar(PM + HIST, HIST), ar(PM + HIST, HIST), ar(at + HIST, HIST),
                                  ALU.subtract).then_inc(s_by, 1)
                dve.wait_ge(s_bh, c.bh.next())
                dve.tensor_tensor(blo[:, 4 + g, 0:TP], ar(PM + HIST, TP), bhi[:, 4 + g, 0:TP].bitcast(F32), ALU.subtract)
                dve.tensor_tensor(blo[:, 4 + g, TP:T], ar(PM + 2 * HIST + TP, TS),
                                  bhi[:, 4 + g, TP:T].bitcast(F32), ALU.subtract).then_inc(s_bl, 1)
                dve.wait_ge(s_bl, c.bl.next() + 1)
                if g % 2 == 0:
                    continue
                for h in (g - 1, g):
                    dve.wait_ge(s_oh, c.oh.next())
                    b = 4 + 2 * (h % 2)
                    gain = par[:, R_SUB + l:R_SUB + l + 1]
                    dve.scalar_tensor_tensor(out=blo[:, 8 + h, 0:TP], in0=ps[:, b, 0:TP], scalar=gain,
                                             in1=bhi[:, 8 + h, 0:TP].bitcast(F32), op0=ALU.mult, op1=ALU.subtract)
                    dve.scalar_tensor_tensor(out=blo[:, 8 + h, TP:T], in0=ps[:, b + 1, 0:TS], scalar=gain,
                                             in1=bhi[:, 8 + h, TP:T].bitcast(F32), op0=ALU.mult,
                                             op1=ALU.subtract).then_inc(s_ol, 1)
            with c.trips(4, **turns(12), **seen(12), pair0=6, pair1=6, step=2, mg=2) as g:
                for d2 in range(2):
                    md = mrg[:, bass.ds(g * 2 + d2, 1), :].rearrange("p a t -> p (a t)")
                    for j in range(6):
                        split(GATE_J, 6 * d2 + j + 2)
                        p = j % 2
                        c.of("pair", p).next()
                        if j in (0, 1, 4):
                            skip(6 * d2 + j)
                            continue
                        ready(6 * d2 + j)
                        if j == 2:
                            dve.wait_ge(free[0], c.of("pair", 0).now())
                            dve.tensor_tensor(halves(md), bank2(0), halves(ar(SA, T)), ALU.mult).then_inc(free[0], 1)
                            dve.wait_ge(free[0], c.of("pair", 0).now() + 1)
                        elif j == 3:
                            dve.wait_ge(free[1], c.of("pair", 1).now())
                            ins = dve.scalar_tensor_tensor(
                                out=halves(ar(GT, T)), in0=bank2(1),
                                scalar=par[:, bass.ds(g * 2 + (R_PS + 8 * l + d2), 1)],
                                in1=halves(ar(SB_, T)), op0=ALU.mult, op1=ALU.mult)
                            ins.then_inc(free[1], 1)
                            dve.wait_ge(free[1], c.of("pair", 1).now() + 1)
                            step(dve.tensor_tensor(md, md, ar(GT, T), ALU.add))
                        else:
                            dve.wait_ge(free[0], c.of("pair", 0).now() + 1)
                            dve.tensor_tensor(halves(ar(GT, T)), bank2(1), halves(ar(SC_, T)), ALU.mult)\
                               .then_inc(free[1], 1)
                            dve.wait_ge(free[1], c.of("pair", 1).now() + 1)
                            dve.tensor_tensor(md, md, ar(GT, T), ALU.add).then_inc(s_mg, 1)
                            dve.wait_ge(s_mg, c.mg.next())
            for k in range(KD):
                dve.wait_ge(s_mh, c.mh.next())
                dve.tensor_tensor(blo[:, k, :], mrg[:, k, :], bhi[:, k, :].bitcast(F32), ALU.subtract).then_inc(s_ml, 1)
            dve.wait_ge(s_tt, l + 1)
            dve.tensor_copy(ar(TROW, 512, 34), ps[0:34, 6, :]).then_inc(s_tk, 1)
            with c.trips(4, **turns(2), **seen(2), pair0=1, pair1=1) as m2:
                for j in range(2):
                    split(OUT_J, j + 2)
                    ready(j)
                    xd = halves(xT[:, bass.ds(m2 * 2 + j, 1), :].rearrange("p a t -> p (a t)"))
                    dve.tensor_tensor(xd, bank2(j), xd, ALU.add).then_inc(free[j], 1)
                    c.of("pair", j).next()
            dve.drain().then_inc(s_xr, 1)
            dve.wait_ge(s_ts, 64 * (l + 1))
            if l:
                dve.wait_ge(s_rw, 1)
                dve.tensor_tensor(selr[:, 64:128], WR.rearrange("p k e -> p (k e)"), selr[:, 0:64].bitcast(F32),
                                  ALU.subtract).then_inc(s_rw, 1)
            norm_dve(R_FFN + 8 * l)
            if l == 0:
                with c.trips(2, **both(turns(2, NF), turns(4, 4), seen(2, NF), seen(4, 4)), pair0=NF + 4,
                             pair1=NF + 4, fh=NF, fl=NF):
                    with c.trips(NF, **turns(2), **seen(2), pair0=1, pair1=1, fh=1, fl=1) as f:
                        split(UP_J, 2)
                        skip(0)
                        split(UP_J, 3)
                        ready(1)
                        dve.wait_ge(free[0], c.of("pair", 0).next() + 1)
                        dve.tensor_tensor(halves(ar(FA, T)), bank2(1), halves(ar(FS, T)), ALU.mult).then_inc(free[1], 1)
                        dve.wait_ge(free[1], c.of("pair", 1).next() + 1)
                        dve.wait_ge(s_fh, c.fh.next())
                        dve.tensor_tensor(blo[:, bass.ds(f, 1), :].rearrange("p a t -> p (a t)"), ar(FA, T),
                                          bhi[:, bass.ds(f, 1), :].rearrange("p a t -> p (a t)").bitcast(F32),
                                          ALU.subtract).then_inc(s_fl, 1)
                        dve.wait_ge(s_fl, c.fl.next())
                    with c.trips(4, **turns(4), **seen(4), pair0=1, pair1=1) as m2:
                        for j in range(4):
                            split(DOWN_J, j + 2)
                            if j < 2:
                                skip(j)
                                continue
                            ready(j)
                            xd = halves(xT[:, bass.ds(m2 * 2 + (j - 2), 1), :].rearrange("p a t -> p (a t)"))
                            dve.tensor_tensor(xd, bank2(j - 2), xd, ALU.add).then_inc(free[j - 2], 1)
                            c.of("pair", j - 2).next()
                dve.drain().then_inc(s_xr, 1)

        dve.wait_ge(s_lge, 1)
        dve.tensor_copy(halves(LGT), ps[0:NE, 0:2, 0:HALF]).then_inc(s_lgk, 1)
        for p in range(AHEAD, AHEAD_E):
            split(EXPERT_J, p)
        dve.wait_ge(s_lg, 1)
        for t in (LG, RM, WT, T1, T2):
            dve.memset(t, 0.0)
        step(dve.memset(EQ, 0.0))
        step(dve.tensor_tensor(LG[:, 0:4, :], ps[:, 0, 0:32].rearrange("p (j e) -> p j e", j=4),
                               BR.rearrange("p (j e) -> p j e", j=1).broadcast_to([P, 4, NE]), ALU.add))
        step(dve.tensor_tensor(LG[0:TS, 4, :], ps[0:TS, 0, 32:40], BR[0:TS, :], ALU.add))

        def e3(ap):
            return ap.rearrange("p (j a) -> p j a", a=1).broadcast_to([P, NTT, NE])
        rank = kc[:, K_RANK:K_RANK + NE].rearrange("p (a e) -> p a e", a=1).broadcast_to([P, NTT, NE])

        def first_max(m, top, oh):
            step(dve.tensor_reduce(top, m, AX, ALU.max))
            step(dve.tensor_tensor(EQ, m, e3(top), ALU.is_equal))
            step(dve.tensor_tensor(EQ, EQ, rank, ALU.mult))
            step(dve.tensor_reduce(R1[3], EQ, AX, ALU.max))
            step(dve.tensor_tensor(oh, EQ, e3(R1[3]), ALU.is_equal))
        first_max(LG, R1[0], OH1)
        step(dve.scalar_tensor_tensor(out=T1, in0=OH1, scalar=BIG, in1=LG, op0=ALU.mult, op1=ALU.add))
        first_max(T1, R1[1], OH2)
        dve.tensor_tensor(R1[2], R1[1], R1[0], ALU.subtract).then_inc(s_re, 1)
        step(dve.tensor_tensor(T2, OH1, OH2, ALU.add))
        dve.tensor_copy(RM[:, 0:4, :], T2[:, 0:4, :])
        dve.tensor_copy(RM[0:TS, 4, :], T2[0:TS, 4, :]).then_inc(s_rt, 1)

        def residual_rows(j):
            n = P if j < 4 else TS
            for g in range(2):
                t = 6 * j + 4 + g
                dve.wait_ge(s_ht, t + 1)
                dve.tensor_copy(xtok[0:n, j, g * 512:(g + 1) * 512], ps[0:n, 2 + t % 4, :]).then_inc(s_hkd, 1)

        for j in range(3):
            residual_rows(j)
        dve.wait_ge(s_rx, 1)
        step(dve.tensor_scalar(R1[3], R1[2], 1.0, None, ALU.add))
        step(dve.reciprocal(R1[3], R1[3]))
        step(dve.tensor_tensor(R1[4], R1[2], R1[3], ALU.mult))
        step(dve.tensor_tensor(T1, OH1, e3(R1[3]), ALU.mult))
        step(dve.tensor_tensor(T2, OH2, e3(R1[4]), ALU.mult))
        step(dve.tensor_tensor(WT, T1, T2, ALU.add))
        dve.wait_ge(s_pos, 1)
        step(dve.memset(SL, -1.0))
        step(dve.tensor_tensor(SL[:, 0:4, :], ps[:, 6, 0:32].rearrange("p (j e) -> p j e", j=4), RM[:, 0:4, :], ALU.mult))
        step(dve.tensor_tensor(SL[0:TS, 4, :], ps[0:TS, 6, 32:40], RM[0:TS, 4, :], ALU.mult))
        step(dve.tensor_scalar(SL[:, 0:4, :], SL[:, 0:4, :], -1.0, None, ALU.add))
        step(dve.tensor_scalar(SL[0:TS, 4, :], SL[0:TS, 4, :], -1.0, None, ALU.add))
        step(dve.tensor_reduce(rmaxc, ps[:, 7, 0:8], AX, ALU.max))
        step(dve.memset(rtmp, 0.0))
        for r in range(1, MAXR):
            step(dve.tensor_scalar(rtmp[:, r - 1:r], rmaxc, float(r * CAP), None, ALU.is_gt))
        step(dve.tensor_reduce(rnd, rtmp, AX, ALU.add))
        step(dve.tensor_scalar(rnd, rnd, 1.0, None, ALU.add))
        dve.tensor_copy(rounds_i[:, 0:1], rnd).then_inc(s_go, 1)
        for j in range(3, NTT):
            residual_rows(j)
        dve.wait_ge(s_go, 1)
        dve.wait_ge(s_hkd, 10)
        rounds = dve.value_load(rounds_i[0:1, 0:1], min_val=1, max_val=MAXR)
        per = both(turns(len(EXPERT_J)), seen(len(EXPERT_J)),
                   dict(pair0=10, pair1=10, pair2=5, pair3=5, gh=8, fh=NF, yh=4, sp=10, fl=NF, sel=1, st=1, si=NF, step=1))
        outer = {k: NE * v for k, v in per.items()}

        def choose(e1):
            for j in range(NTT):
                n = P if j < 4 else TS
                ins = dve.tensor_scalar(sel[0:n, j, :], kc[0:n, K_IOTA:K_IOTA + CAP], SL[0:n, j, e1], None,
                                        ALU.is_equal)
            ins.then_inc(s_sel, 1)
            dve.wait_ge(s_sel, c.sel.next())
            step(dve.tensor_scalar(SL[:, :, e1], SL[:, :, e1], float(CAP), None, ALU.subtract))

        def hidden_lo(f):
            dve.wait_ge(s_fh, c.fh.next())
            dve.tensor_tensor(ea[:, 1, f, :], ar(EA + CAP * (f % 2), CAP), ea[:, 0, f, :].bitcast(F32),
                              ALU.subtract).then_inc(s_fl, 1)
            c.fl.next()

        def both_halves(out, b):
            return dve.tensor_reduce(out, ps[:, b, 0:2 * CAP].rearrange("p (i c) -> p c i", i=2), AX, ALU.add)

        choose(slice(0, 1))
        with c.trips(rounds, **outer):
            with c.trips(NE, **per) as e:
                e1 = bass.ds(e, 1)
                for d in range(KD):
                    dve.wait_ge(s_gh, c.gh.next())
                    dve.tensor_tensor(hg[:, 1, d, :], ps[:, GATHER[d % 4], 0:CAP], hg[:, 0, d, :].bitcast(F32),
                                      ALU.subtract).then_inc(s_gl, 1)
                for f in range(NF):
                    p = 2 * (f % 2)
                    gate, hidden = ar(ES + CAP * (f % 2), CAP), ar(EA + CAP * (f % 2), CAP)
                    ready(2 * f)
                    both_halves(gate, p).then_inc(free[p], 1)
                    c.of("pair", p).next()
                    split(EXPERT_J, 2 * f + AHEAD_E)
                    if f:
                        hidden_lo(f - 1)
                    ready(2 * f + 1)
                    both_halves(hidden, p + 1).then_inc(free[p + 1], 1)
                    dve.wait_ge(free[p + 1], c.of("pair", p + 1).next() + 1)
                    dve.wait_ge(s_si, c.si.next())
                    dve.tensor_tensor(hidden, hidden, gate, ALU.mult).then_inc(s_em, 1)
                    split(EXPERT_J, 2 * f + 1 + AHEAD_E)
                hidden_lo(NF - 1)
                for m2 in range(4):
                    for q in range(4):
                        j = 2 * NF + 4 * m2 + q
                        if q < 2:
                            skip(j)
                        else:
                            ready(j)
                            both_halves(yT[:, 2 * m2 + q - 2, :], q - 2).then_inc(free[q - 2], 1)
                            c.of("pair", q - 2).next()
                        for i in ((0,), (), (), (1, 2, 3) if m2 < 3 else (1,))[q]:
                            split(EXPERT_J, refill(2 * NF + 4 * m2 + i))
                    if m2 == 1:
                        dve.wait_ge(s_st, c.st.next())
                        choose(bass.ds((e + 1) % NE, 1))
                for g in range(2):
                    for a, cn in enumerate(CAPT):
                        dve.wait_ge(s_yh, c.yh.next())
                        at = slice(g * 512, (g + 1) * 512)
                        dve.tensor_tensor(ey[0:cn, 1, a, at], ps[0:cn, 4 + 2 * a + g, :],
                                          ey[0:cn, 0, a, at].bitcast(F32), ALU.subtract).then_inc(s_yl, 1)
                for j in (-2, -1):
                    split(EXPERT_J, refill(len(EXPERT_J) + j))
                for n in range(2 * NTT):
                    g, j = divmod(n, NTT)
                    rows_ = P if j < 4 else TS
                    dve.wait_ge(s_sp, c.sp.next())
                    xd = xtok[0:rows_, j, g * 512:(g + 1) * 512]
                    dve.scalar_tensor_tensor(out=xd, in0=ps[0:rows_, SPREAD[n % 4], :], scalar=WT[0:rows_, j, e1],
                                             in1=xd, op0=ALU.mult, op1=ALU.add).then_inc(s_acc, 1)
        dve.drain().then_inc(s_mix, 1)
        dve.wait_ge(s_fsq, 1)
        dve.tensor_scalar(frms, fsum, 1.0 / D, EPS, ALU.mult, ALU.add).then_inc(s_ms, 1)
        dve.wait_ge(s_frm, 1)
        dve.reciprocal(frms, frms).then_inc(s_frm, 1)
        dve.wait_ge(s_frm, 2)
        dve.wait_ge(s_gf, 16)
        for j in range(NTT):
            n = P if j < 4 else TS
            dve.scalar_tensor_tensor(out=xtok[0:n, j, :], in0=xtok[0:n, j, :], scalar=frms[0:n, j:j + 1],
                                     in1=ar(GF, D, n), op0=ALU.mult, op1=ALU.mult).then_inc(s_fin, 1)

    ctx.close()


_INS = ['x_prompt', 'x_sample', 'cache_k', 'cache_v', 'state_conv', 'state_pool', 'norm_mix', 'w_in', 'conv_w',
        'w_conv_out', 'w_pool', 'pool_scale', 'lambda_q1', 'lambda_k1', 'lambda_q2', 'lambda_k2', 'subln_g',
        'w_attn_out', 'w_o', 'norm_ffn', 'w_gate_d', 'w_up_d', 'w_down_d', 'w_router', 'b_router', 'w_gate_e',
        'w_up_e', 'w_down_e', 'norm_final']
_OUTS = [(1, 512, 1024), (1, 32, 1024), (2, 1, 512, 4, 128), (2, 1, 512, 4, 128), (2, 1, 2, 512), (2, 1, 15, 512),
         (2, 1, 32, 4, 128), (2, 1, 32, 4, 128), (2, 1, 2, 512), (2, 1, 15, 512)]


def constants(np):
    k = np.zeros((P, K_N), np.float32)
    pos = np.concatenate([np.arange(TP), PAST + np.arange(TS)]).astype(np.float32)
    half = 32
    freq = np.float32(10000.0) ** (-np.arange(half, dtype=np.float32) / np.float32(half))
    ang = (freq[:, None].astype(np.float32) * pos[None, :]).astype(np.float32)
    k[:, K_COS:K_COS + T] = np.tile(np.cos(ang), (4, 1))
    k[:, K_SIN:K_SIN + T] = np.tile(np.sin(ang), (4, 1))
    k[:, K_ID:K_ID + P] = np.eye(P)
    for p in range(P):
        if p % 64 < 32:
            k[p + 32, K_ROT + p] = -1.0
        else:
            k[p - 32, K_ROT + p] = 1.0
    k[:, K_TRI:K_TRI + P] = np.triu(np.ones((P, P)))
    k[:, K_IOTA:K_IOTA + CAP] = np.arange(CAP)[None, :]
    for g in range(4):
        k[:, K_RC + HIST * g:K_RC + HIST * (g + 1)] = 1.0 / np.minimum(np.arange(HIST) + 1, 2 ** (g + 1))
    k[:, K_RANK:K_RANK + NE] = NE - np.arange(NE)
    return k


def kernel(**inputs):
    import numpy as _np
    import concourse.bacc as _bacc
    from concourse import mybir as _mybir
    from concourse.bass_utils import run_bass_kernel_spmd as _run

    nc = _bacc.Bacc("TRN2", target_bir_lowering=False, num_devices=1)
    arrays, args = {}, []
    for name in _INS:
        a = _np.ascontiguousarray(inputs[name])
        arrays[f"in_{name}_dram"] = a
        args.append(nc.dram_tensor(f"in_{name}_dram", a.shape, _mybir.dt.from_np(a.dtype), kind="ExternalInput").ap())
    a = constants(_np)
    arrays["in_consts_dram"] = a
    args.append(nc.dram_tensor("in_consts_dram", a.shape, _mybir.dt.float32, kind="ExternalInput").ap())
    for i, shape in enumerate(_OUTS):
        args.append(nc.dram_tensor(f"out_{i}_dram", shape, _mybir.dt.float32, kind="ExternalOutput").ap())
    program(nc, *args)
    r = _run(nc, [arrays], core_ids=[0])
    return tuple(r.results[0][f"out_{i}_dram"] for i in range(len(_OUTS)))
```
